# Optimizing a Trainium2 kernel written in Bass

```python
import math
import jax, jax.numpy as jnp
from jax import lax
import numpy as np

D_MODEL = 1024
BATCH = 1
SEQ = 1024
DEPTH = 1

CHUNK = 64
N_MIXERS = 2
N_FOX = (DEPTH + N_MIXERS - 1) // N_MIXERS
N_S5 = DEPTH // N_MIXERS
FOX_HEADS = 16
FOX_HEAD_DIM = 64
FOX_WIDTH = FOX_HEADS * FOX_HEAD_DIM
Q_BLOCK = 128
FORGET_BIAS_INIT = 2.0
S5_WIDTH = D_MODEL
S5_GROUP = 16
S5_GROUPS = S5_WIDTH // S5_GROUP
S5_STATE = 64
DT_MIN = 1e-3
DT_MAX = 1e-1
PLE_DIM = 256
RMS_EPS = 1e-6
NEG_INF = -1e30

kernel_name = "fox_s5_interleaved_sandwich_ple"

def rmsnorm(x, g):
    xf = x.astype(jnp.float32)
    var = jnp.mean(xf * xf, axis=-1, keepdims=True)
    return (xf * lax.rsqrt(var + RMS_EPS) * g.astype(jnp.float32)).astype(x.dtype)

def fox_mixer(h, w_in, b_f, w_out):
    bsz, seq, _ = h.shape
    proj = h @ w_in
    q, k, v, z, fl = jnp.split(
        proj, [FOX_WIDTH, 2 * FOX_WIDTH, 3 * FOX_WIDTH, 4 * FOX_WIDTH], axis=-1)
    q = q.reshape(bsz, seq, FOX_HEADS, FOX_HEAD_DIM)
    k = k.reshape(bsz, seq, FOX_HEADS, FOX_HEAD_DIM)
    v = v.reshape(bsz, seq, FOX_HEADS, FOX_HEAD_DIM)
    log_f = jax.nn.log_sigmoid(fl.astype(jnp.float32) + b_f.astype(jnp.float32))
    cum = jnp.cumsum(log_f, axis=1).transpose(0, 2, 1)
    scale = FOX_HEAD_DIM ** -0.5
    outs = []
    for start in range(0, seq, Q_BLOCK):
        end = start + Q_BLOCK
        s = jnp.einsum('bqhd,bkhd->bhqk', q[:, start:end], k[:, :end]).astype(jnp.float32) * scale
        bias = cum[:, :, start:end, None] - cum[:, :, None, :end]
        qpos = jnp.arange(start, end)[:, None]
        kpos = jnp.arange(end)[None, :]
        logits = jnp.where(kpos <= qpos, s + bias, NEG_INF)
        pr = jax.nn.softmax(logits, axis=-1)
        outs.append(jnp.einsum('bhqk,bkhd->bqhd', pr.astype(v.dtype), v[:, :end]))
    o = jnp.concatenate(outs, axis=1).reshape(bsz, seq, FOX_WIDTH)
    return (o * jax.nn.silu(z)) @ w_out

def _ssm_combine(e1, e2):
    a1r, a1i, b1r, b1i = e1
    a2r, a2i, b2r, b2i = e2
    ar = a2r * a1r - a2i * a1i
    ai = a2r * a1i + a2i * a1r
    br = a2r * b1r - a2i * b1i + b2r
    bi = a2r * b1i + a2i * b1r + b2i
    return (ar, ai, br, bi)

def s5_mixer(h, w_in, lam_re, lam_im, log_dt, b_re, b_im, c_re, c_im, d_skip, w_glu, b_glu, w_out):
    bsz, seq, _ = h.shape
    f32 = jnp.float32
    proj = h @ w_in
    u, z = jnp.split(proj, [S5_WIDTH], axis=-1)
    u32 = u.astype(f32).reshape(bsz, seq, S5_GROUPS, S5_GROUP)
    lr = lam_re.astype(f32)
    li = lam_im.astype(f32)
    dt = jnp.exp(log_dt.astype(f32))[:, None]
    mag = jnp.exp(lr * dt)
    lb_re = mag * jnp.cos(li * dt)
    lb_im = mag * jnp.sin(li * dt)
    den = lr * lr + li * li
    num_re = lb_re - 1.0
    num_im = lb_im
    coef_re = (num_re * lr + num_im * li) / den
    coef_im = (num_im * lr - num_re * li) / den
    br = b_re.astype(f32)
    bi = b_im.astype(f32)
    bb_re = coef_re[..., None] * br - coef_im[..., None] * bi
    bb_im = coef_re[..., None] * bi + coef_im[..., None] * br
    bu_re = jnp.einsum('blgi,gpi->lbgp', u32, bb_re)
    bu_im = jnp.einsum('blgi,gpi->lbgp', u32, bb_im)
    a_re = jnp.broadcast_to(lb_re[None, None], (seq, 1, S5_GROUPS, S5_STATE))
    a_im = jnp.broadcast_to(lb_im[None, None], (seq, 1, S5_GROUPS, S5_STATE))
    _, _, h_re, h_im = lax.associative_scan(_ssm_combine, (a_re, a_im, bu_re, bu_im), axis=0)
    y = (jnp.einsum('lbgp,gip->blgi', h_re, c_re.astype(f32))
         - jnp.einsum('lbgp,gip->blgi', h_im, c_im.astype(f32)))
    y = y.reshape(bsz, seq, S5_WIDTH) + d_skip.astype(f32) * u.astype(f32)
    y = y.astype(h.dtype)
    g = jax.nn.gelu(y)
    y = g * jax.nn.sigmoid(g @ w_glu + b_glu)
    return (y * jax.nn.silu(z)) @ w_out

def setup_inputs(seed: int = 0) -> dict:
    key = jax.random.key(seed)
    ks = jax.random.split(key, 24)
    nrm = jax.random.normal
    d = D_MODEL
    x = nrm(ks[0], (BATCH, SEQ, d), jnp.float32)
    p = nrm(ks[1], (DEPTH, BATCH, SEQ, PLE_DIM), jnp.float32)
    ln_pre = 1.0 + 0.05 * nrm(ks[2], (DEPTH, d), jnp.float32)
    ln_post = 1.0 + 0.05 * nrm(ks[3], (DEPTH, d), jnp.float32)
    fox_w_in = nrm(ks[4], (N_FOX, d, 4 * FOX_WIDTH + FOX_HEADS), jnp.float32) * d ** -0.5
    fox_b_f = FORGET_BIAS_INIT + 0.5 * nrm(ks[5], (N_FOX, FOX_HEADS), jnp.float32)
    fox_w_out = nrm(ks[6], (N_FOX, FOX_WIDTH, d), jnp.float32) * FOX_WIDTH ** -0.5
    s5_w_in = nrm(ks[7], (N_S5, d, 2 * S5_WIDTH), jnp.float32) * d ** -0.5
    s5_lambda_re = -0.5 * jnp.exp(0.02 * nrm(ks[8], (N_S5, S5_GROUPS, S5_STATE), jnp.float32))
    s5_lambda_im = (math.pi * jnp.arange(S5_STATE, dtype=jnp.float32)[None, None, :]
                    + 0.01 * nrm(ks[9], (N_S5, S5_GROUPS, S5_STATE), jnp.float32))
    s5_log_dt = jax.random.uniform(ks[10], (N_S5, S5_GROUPS), jnp.float32,
                                   minval=math.log(DT_MIN), maxval=math.log(DT_MAX))
    bscale = (2.0 * S5_GROUP) ** -0.5
    s5_b_re = nrm(ks[11], (N_S5, S5_GROUPS, S5_STATE, S5_GROUP), jnp.float32) * bscale
    s5_b_im = nrm(ks[12], (N_S5, S5_GROUPS, S5_STATE, S5_GROUP), jnp.float32) * bscale
    cscale = S5_STATE ** -0.5
    s5_c_re = nrm(ks[13], (N_S5, S5_GROUPS, S5_GROUP, S5_STATE), jnp.float32) * cscale
    s5_c_im = nrm(ks[14], (N_S5, S5_GROUPS, S5_GROUP, S5_STATE), jnp.float32) * cscale
    s5_d = nrm(ks[15], (N_S5, S5_WIDTH), jnp.float32)
    s5_w_glu = nrm(ks[16], (N_S5, S5_WIDTH, S5_WIDTH), jnp.float32) * S5_WIDTH ** -0.5
    s5_b_glu = 0.01 * nrm(ks[17], (N_S5, S5_WIDTH), jnp.float32)
    s5_w_out = nrm(ks[18], (N_S5, S5_WIDTH, d), jnp.float32) * S5_WIDTH ** -0.5
    ple_w_proj = nrm(ks[19], (DEPTH, PLE_DIM, d), jnp.float32) * PLE_DIM ** -0.5
    ple_w_gate = nrm(ks[20], (DEPTH, d, d), jnp.float32) * d ** -0.5
    ple_b_gate = 0.01 * nrm(ks[21], (DEPTH, d), jnp.float32)
    return {"x": x, "p": p, "ln_pre": ln_pre, "ln_post": ln_post,
            "fox_w_in": fox_w_in, "fox_b_f": fox_b_f, "fox_w_out": fox_w_out,
            "s5_w_in": s5_w_in, "s5_lambda_re": s5_lambda_re, "s5_lambda_im": s5_lambda_im,
            "s5_log_dt": s5_log_dt, "s5_b_re": s5_b_re, "s5_b_im": s5_b_im,
            "s5_c_re": s5_c_re, "s5_c_im": s5_c_im, "s5_d": s5_d,
            "s5_w_glu": s5_w_glu, "s5_b_glu": s5_b_glu, "s5_w_out": s5_w_out,
            "ple_w_proj": ple_w_proj, "ple_w_gate": ple_w_gate, "ple_b_gate": ple_b_gate}

def reference(x, p, ln_pre, ln_post, fox_w_in, fox_b_f, fox_w_out, s5_w_in, s5_lambda_re,
              s5_lambda_im, s5_log_dt, s5_b_re, s5_b_im, s5_c_re, s5_c_im, s5_d, s5_w_glu,
              s5_b_glu, s5_w_out, ple_w_proj, ple_w_gate, ple_b_gate):
    for i in range(DEPTH):
        h = rmsnorm(x, ln_pre[i])
        j = i // N_MIXERS
        if i % N_MIXERS == 0:
            y = fox_mixer(h, fox_w_in[j], fox_b_f[j], fox_w_out[j])
        else:
            y = s5_mixer(h, s5_w_in[j], s5_lambda_re[j], s5_lambda_im[j], s5_log_dt[j],
                         s5_b_re[j], s5_b_im[j], s5_c_re[j], s5_c_im[j], s5_d[j],
                         s5_w_glu[j], s5_b_glu[j], s5_w_out[j])
        x = x + rmsnorm(y, ln_post[i])
        gate = jax.nn.sigmoid(x @ ple_w_gate[i] + ple_b_gate[i])
        x = x + (p[i] @ ple_w_proj[i]) * gate
    return x


_drawn_inputs = setup_inputs


def setup_inputs(seed=0):
    import zlib

    import numpy as np

    out = dict(_drawn_inputs(seed))
    spreads = {}
    factors = {'ple_b_gate': 43.449}
    for name, (base, spread) in spreads.items():
        noise = np.random.default_rng([zlib.crc32(name.encode()), seed]).standard_normal(out[name].shape)
        drawn = base * np.exp(spread * noise) if base else spread * noise
        out[name] = __import__('jax').numpy.asarray(drawn.astype(out[name].dtype))
    for name, factor in factors.items():
        out[name] = (out[name] * factor).astype(out[name].dtype)
    return out
```

```python
from contextlib import ExitStack

import numpy as np

import concourse.bass as bass
from concourse import mybir
from concourse.alu_op_type import AluOpType as ALU

F32 = mybir.dt.float32
F32R = mybir.dt.float32r
BF16 = mybir.dt.bfloat16
ACT = mybir.ActivationFunctionType

P = 128
D = 1024
T = 1024
KT = D // P
TT = T // P
HEADS = 16
HD = 64
PAIRS = HEADS // 2
QUADS = HEADS // 4
VC = 4 * HD + 4
PLE = 256
PK = PLE // P
EPS = 1e-6
NEG = -1e30
BIG = 3e38
HALF = 512
GW = 256
GROUPS = T // GW
UNITS = 2 * GROUPS
SCALE = HD ** -0.5
MMS = 3
W_HALF = (0, 1, 0)
M_HALF = (0, 0, 1)
BLOCK = KT * MMS
QK_BLOCKS = 4

U_Z = 2 * PAIRS
U_Y = U_Z + KT
U_G = U_Y + KT
U_END = U_G + KT

CHUNKS = [(g, r, c) for g in range(GROUPS) for r in range(2) for c in range(g + 1)]
NCH = len(CHUNKS)
LAG = CHUNKS.index((GROUPS - 1, 0, 0))


def chunks_until(g, r):
    return CHUNKS.index((g, r, g)) + 1


FILL = (6, 8, 10, 12, 12, 12, 12, 24)
FILL_TO = [sum(FILL[:j + 1]) for j in range(TT)]


def step_order(first=False, last=False):
    def chunks_of(j):
        g = GROUPS - 1 if j < 2 else (j - 2) // 2
        back = int(j < 2)
        return [] if first and back else [(back, n) for n, (a, r, _) in enumerate(CHUNKS) if (a, r) == (g, j % 2)]

    order, filled = [], 0

    def fill(until):
        nonlocal filled
        while filled < until and not last:
            m1 = min(until, (filled // BLOCK + 1) * BLOCK)
            order.append(("fill", filled, m1))
            filled = m1
            if filled % BLOCK == 0:
                order.append(("block", filled // BLOCK - 1))

    if first:
        fill(BLOCK)
    for j in range(TT):
        mine = chunks_of(j)
        following = chunks_of(j + 1) if j % 2 == 0 else []
        order.append(("logits", j))
        start, parts = filled, len(mine) + 1
        share = lambda q: start + max(0, FILL_TO[j] - start) * q // parts
        order.append(("take", j, 0))
        if j % 2 == 0 and mine:
            fill(share(1))
            order.append(("turn", *mine[0]))
        order += [("take", j, 1), ("exp", j, 0)]
        if j % 2:
            order.append(("scale", j - 1))
        for q, chunk in enumerate(mine):
            for ahead in (mine + following)[q + 1:q + 2]:
                order.append(("turn", *ahead))
            if q == 0:
                order.append(("exp", j, 1))
            fill(share(q + 2))
            order.append(("weigh", *chunk))
        if not mine:
            order.append(("exp", j, 1))
        fill(FILL_TO[j])
        if j % 2:
            order.append(("scale", j))
    return order


TAIL = [("turn", 0, LAG)] + [x for n in range(LAG, NCH) for x in
        ([("turn", 0, n + 1)] if n + 1 < NCH else []) +
        [("fill", (n - LAG) * 2 * BLOCK // (NCH - LAG), (n + 1 - LAG) * 2 * BLOCK // (NCH - LAG)), ("weigh", 0, n)]]


def key_width(j):
    w = (j + 1) * P
    return w, (1 if w <= HALF else 2)


PLACES = 4
PLACE_W = [(TT - PLACES + 1 + s) * P for s in range(PLACES)]
PLACE_AT = [sum(PLACE_W[:s]) for s in range(PLACES)]
HEAD_W = sum(PLACE_W)


def build(nc, x_nat, x_t, wv, w_all, w_ple, p_t, f_bias, g_pre, g_post, b_gate, scratch, out_t):
    with ExitStack() as ctx:
        def sb(name, shape, dt):
            return ctx.enter_context(nc.sbuf_tensor(name, shape, dt))

        def sem(name):
            return ctx.enter_context(nc.semaphore(name))

        xh = sb("xh", [P, KT, T], F32R)
        xl = sb("xl", [P, KT, T], F32R)
        qk = sb("qk", [P, 2, 4, T], F32R)
        vs = sb("vs", [P, TT, 2, P], F32R)
        pt = sb("pt", [P, 2, 2, 2, GW], F32R)
        wraw = sb("wraw", [P, KT * P], F32)
        wsp = sb("wsp", [P, 2, 2, KT * P], F32R)
        vo = sb("vo", [P, PAIRS, T], F32)
        lp = sb("lp", [P, 2 * HEAD_W], F32)
        cb = sb("cb", [P, 2, T], F32)
        rstd_b = sb("rstd_b", [P, T], F32)
        ident = sb("ident", [P, P], F32)
        ident16 = sb("ident16", [P, P], BF16)
        mask16 = sb("mask16", [P, P], BF16)
        ones = sb("ones", [P, P], F32)
        zeros = sb("zeros", [P, P], F32)
        fl = sb("fl", [P, TT, HEADS], F32)
        vecs = sb("vecs", [P, 3, KT], F32)
        bf = sb("bf", [HEADS, 1], F32)
        col = sb("col", [P, 4, TT], F32)
        nmax = sb("nmax", [P, 2 * TT], F32)
        rsum = sb("rsum", [P, 2 * TT], F32)
        rinv = sb("rinv", [P, 2 * TT], F32)
        oc = sb("oc", [P, 2, GW], F32)
        ps = ctx.enter_context(nc.psum_tensor("ps", [P, 8, HALF], F32))
        SB, TB, OB, PB = 0, 4, 6, 7

        g_pre_sb, g_post_sb, b_gate_sb = (vecs[:, i, :] for i in range(3))
        wv_raw = [lp[:, i * KT * VC:(i + 1) * KT * VC].rearrange("p (k n) -> p k n", k=KT) for i in range(2)]
        x_nat_sb = [lp[:, 2 * KT * VC:2 * KT * VC + D], cb[:, 0, :]]
        square_out = cb[:, 1, :]
        wv_sp = qk[:].rearrange("p a b t -> p (a b t)")[:, 0:KT * 2 * VC].rearrange("p (k h n) -> p k h n", k=KT, h=2)
        diag = lp[:, 2 * HEAD_W - TT * P:].rearrange("p (t n) -> p t n", t=TT)
        gate_work = [lp[0:HEADS, i * T:(i + 1) * T] for i in range(4)]
        work = [lp[:, i * T:(i + 1) * T] for i in range(2)]
        x_res = [lp[:, (2 + i) * T:(3 + i) * T] for i in range(2)]
        ple_raw = [lp[:, 4 * T + i * PK * P:4 * T + (i + 1) * PK * P] for i in range(2)]
        ple_sp = vs[:].rearrange("p a b n -> p (a b n)")[:, 0:4 * PK * P].rearrange("p (i h n) -> p i h n", i=2, h=2)
        p_sp = qk[:, 0, :, :].rearrange("p (h k) t -> p h k t", h=2)
        sq_sum = cb[:, 0, :]

        def f32(ap):
            return ap.bitcast(F32)

        def banks(bank, n=2):
            return ps[:, bank:bank + n, :].rearrange("p b n -> p (b n)")

        def lp_at(r, j):
            at = r * HEAD_W + PLACE_AT[j % PLACES]
            return lp[:, at:at + (j + 1) * P]

        x_in = [sem(f"x_in{k}") for k in range(KT)]
        x_nat_in = [sem(f"x_nat_in{i}") for i in range(2)]
        wv_in = [sem(f"wv_in{i}") for i in range(2)]
        x_res_in = [sem(f"x_res_in{i}") for i in range(2)]
        ple_in = [sem(f"ple_in{i}") for i in range(2)]
        out_done = [sem(f"out_done{i}") for i in range(2)]
        p_in = [sem(f"p_in{i}") for i in range(PK)]
        (vecs_in, w_in, cb_in, gates_out) = map(sem, ("vecs_in", "w_in", "cb_in", "gates_out"))
        (zeros_set, const_set, x_hi, x_lo, wv_hi, wv_lo, wv_used, v_ready, v_used_act, v_used_dve) = map(sem, (
            "zeros_set", "const_set", "x_hi", "x_lo", "wv_hi", "wv_lo", "wv_used", "v_ready", "v_used_act", "v_used_dve"))
        (squares, col_act, col_dve, diag_set, rstd_spread, rstd_set, fl_turned, gate_act, gate_dve) = map(sem, (
            "squares", "col_act", "col_dve", "diag_set", "rstd_spread", "rstd_set", "fl_turned", "gate_act", "gate_dve"))
        (w_hi, w_lo, block_ready, block_scaled, block_hi, block_lo) = map(sem, (
            "w_hi", "w_lo", "block_ready", "block_scaled", "block_hi", "block_lo"))
        (logits_ready, logits_set, probs_set, sums_inverted, probs_scaled) = map(sem, (
            "logits_ready", "logits_set", "probs_set", "sums_inverted", "probs_scaled"))
        (turned, pt_hi, pt_lo, pv_done, o_copied, o_added, vs_hi, vs_lo) = map(sem, (
            "turned", "pt_hi", "pt_lo", "pv_done", "o_copied", "o_added", "vs_hi", "vs_lo"))
        (chunk_ready, z_scaled, z_sig, z_mul, oz_set, oz_hi, oz_lo, p_hi, p_lo) = map(sem, (
            "chunk_ready", "z_scaled", "z_sig", "z_mul", "oz_set", "oz_hi", "oz_lo", "p_hi", "p_lo"))
        (y_set, sq_set, sq_added, sum_ready, x1_scaled, x1_set, x1_hi, x1_lo) = map(sem, (
            "y_set", "sq_set", "sq_added", "sum_ready", "x1_scaled", "x1_set", "x1_hi", "x1_lo"))
        (ple_hi, ple_lo, ple_ready, g_sig, g_mul, g_add, sq_clear) = map(sem, (
            "ple_hi", "ple_lo", "ple_ready", "g_sig", "g_mul", "g_add", "sq_clear"))
        act_passed, dve_passed, pool_passed = map(sem, ("act_passed", "dve_passed", "pool_passed"))
        block = ctx.enter_context(nc.Block())

        def later(c):
            return not (isinstance(c, int) and c < 2)

        def wait_apart(eng, passed):
            eng.sem_inc(passed, 1)

        @block.sync
        def _(sp):
            def load_w(u, first=False):
                if not first:
                    sp.wait_ge(w_lo, u)
                sp.dma_start(wraw[:], w_all[bass.ds(u, 1), :, :].rearrange("o p n -> p (o n)")).then_inc(w_in, 16)

            def load_gates(pr):
                for r in range(2):
                    sp.dma_start(cb[:, r, :], scratch[bass.ds(pr * 2 + r, 1), :].to_broadcast([P, T])).then_inc(cb_in, 16)

            for i, v in enumerate((g_pre, g_post, b_gate)):
                sp.dma_start(vecs[:, i, :], v).then_inc(vecs_in, 16)
            sp.dma_start(bf[:], f_bias).then_inc(vecs_in, 16)
            sp.dma_start(vo[:, 0, :], x_t[0, :, :]).then_inc(x_in[0], 16)
            sp.dma_start(wv_raw[0], wv[0, :, :, :]).then_inc(wv_in[0], 16)
            for k in range(1, KT):
                sp.dma_start(vo[:, k, :], x_t[k, :, :]).then_inc(x_in[k], 16)
            sp.dma_start(wv_raw[1], wv[1, :, :, :]).then_inc(wv_in[1], 16)
            load_w(0, first=True)
            for t in range(TT):
                if t >= 2:
                    sp.wait_ge(squares, t - 1)
                sp.dma_start(x_nat_sb[t % 2], x_nat[t, :, :]).then_inc(x_nat_in[t % 2], 16)
            for c in range(2, QUADS):
                sp.wait_ge(wv_lo, (c - 1) * KT // 2)
                sp.dma_start(wv_raw[c % 2], wv[c, :, :, :]).then_inc(wv_in[c % 2], 16)
            load_w(1)
            sp.wait_ge(gate_dve, 6)
            sp.dma_start(scratch, gate_work[0]).then_inc(gates_out, 16)
            sp.wait_ge(gates_out, 16)
            load_gates(0)
            load_w(2)
            load_w(3)
            with sp.Fori(0, PAIRS - 1) as pr:
                load_w(pr * 2 + 4)
                load_w(pr * 2 + 5)
                sp.wait_ge(logits_set, (pr + 1) * 2 * TT)
                load_gates(pr + 1)
            sp.wait_ge(logits_set, PAIRS * 2 * TT)
            for k in range(PK):
                sp.dma_start(cb[:, k, :], p_t[k, :, :]).then_inc(p_in[k], 16)
            with sp.Fori(U_Z + 2, U_G + 2) as u:
                load_w(u)
            sp.wait_ge(sq_added, KT)

            def load_ple(c, par):
                if later(c):
                    sp.wait_ge(ple_lo, c - 1)
                sp.dma_start(ple_raw[par], w_ple[bass.ds(c, 1), :, :].rearrange("o p n -> p (o n)")).then_inc(ple_in[par], 16)

            load_ple(0, 0)
            load_ple(1, 1)
            for c in range(KT):
                if c >= 2:
                    sp.wait_ge(x1_set, c - 1)
                sp.dma_start(x_res[c % 2], x_t[c, :, :]).then_inc(x_res_in[c % 2], 16)

            def store(c, par):
                sp.wait_ge(g_add, c + 1)
                sp.dma_start(out_t[bass.ds(c, 1), :, :].rearrange("o p n -> p (o n)"), work[par]).then_inc(out_done[par], 16)

            with sp.Fori(0, KT // 2 - 1) as i:
                for h in range(2):
                    load_w(i * 2 + U_G + 2 + h)
                    load_ple(i * 2 + 2 + h, h)
                    store(i * 2 + h, h)
            for c in (KT - 2, KT - 1):
                store(c, c % 2)
            for par in range(2):
                sp.wait_ge(out_done[par], KT // 2 * 16)

        @block.gpsimd
        def _(pool):
            nc.gpsimd.memset(zeros[:], 0.0).then_inc(zeros_set, 1)
            nc.gpsimd.memset(ones[:], 1.0).then_inc(const_set, 1)
            pool.wait_ge(zeros_set, 1)
            nc.gpsimd.affine_select(out=ident[:], in_=zeros[:], compare_op=ALU.not_equal, fill=1.0, base=0,
                                    pattern=[[-1, P]], channel_multiplier=1).then_inc(const_set, 1)
            nc.gpsimd.affine_select(out=mask16[:], in_=zeros[:], compare_op=ALU.is_ge, fill=NEG, base=0,
                                    pattern=[[-1, P]], channel_multiplier=1).then_inc(const_set, 1)
            pool.wait_ge(const_set, 2)
            nc.gpsimd.tensor_copy(ident16[:], ident[:]).then_inc(const_set, 1)

            def w_split(u, par):
                pool.wait_ge(w_hi, u + 1)
                nc.gpsimd.tensor_tensor(wsp[:, par, 1, :], wraw[:], f32(wsp[:, par, 0, :]), ALU.subtract).then_inc(w_lo, 1)

            for u in range(3):
                w_split(u, u % 2)

            def v_split(pr, first):
                if not first:
                    pool.wait_ge(o_added, pr * UNITS)
                for i, (t0, t1) in enumerate(((0, 2), (2, TT))):
                    pool.wait_ge(vs_hi, pr * 2 + i + 1)
                    src = vo[:, bass.ds(pr, 1), t0 * P:t1 * P].rearrange("p o (s d) -> p (o s) d", d=HD)
                    v = vs[:, t0:t1, :, :].rearrange("p t r d -> p (t r) d")
                    wait_apart(pool, pool_passed)
                    nc.gpsimd.tensor_tensor(v[:, :, HD:P], src, f32(v[:, :, 0:HD]), ALU.subtract).then_inc(vs_lo, 1)

            def o_add(pr, n, split):
                g, r, c = CHUNKS[n]
                if c < g:
                    return
                head = slice(HD * r, HD * r + HD)
                pool.wait_ge(*split)
                pool.wait_ge(o_copied, pr * UNITS + 2 * g + r + 1)
                dst = vo[head, bass.ds(pr, 1), g * GW:(g + 1) * GW].rearrange("p o n -> p (o n)")
                wait_apart(pool, pool_passed)
                nc.gpsimd.tensor_tensor(dst, oc[head, 0, :], oc[head, 1, :], ALU.add).then_inc(o_added, 1)

            def step(pr, first=False, last=False):
                for what, *a in step_order(first, last):
                    if what == "logits":
                        if a[0] == 0:
                            if not first:
                                pool.wait_ge(o_added, pr * UNITS - 2)
                            w_split(pr * 2 + 3, 1)
                            split = w_lo, pr * 2 + 4
                        if a[0] == 2:
                            v_split(pr, first)
                            split = vs_lo, pr * 2 + 2
                        if a[0] == 5 and not last:
                            pool.wait_ge(o_added, pr * UNITS + 3)
                            w_split(pr * 2 + 4, 0)
                            split = w_lo, pr * 2 + 5
                    elif what == "weigh":
                        o_add(pr - a[0], a[1], split)

            step(0, first=True)
            with pool.Fori(1, PAIRS - 1) as pr:
                step(pr)
            step(PAIRS - 1, last=True)
            for what, *a in TAIL:
                if what == "weigh":
                    o_add(PAIRS - 1, a[1], (vs_lo, PAIRS * 2))

            pool.wait_ge(o_added, PAIRS * UNITS)

            def gate_o(c, par):
                w_split(c + U_Z + 2, par)
                pool.wait_ge(z_mul, c + 1)
                o = vo[:, bass.ds(c, 1), :].rearrange("p o n -> p (o n)")
                wait_apart(pool, pool_passed)
                nc.gpsimd.tensor_tensor(o, o, work[par], ALU.mult).then_inc(oz_set, 1)

            with pool.Fori(0, KT // 2) as i:
                for h in range(2):
                    gate_o(i * 2 + h, h)
            with pool.Fori(0, KT // 2) as i:
                for h in range(2):
                    w_split(i * 2 + h + U_Y + 2, h)
            for c in range(KT):
                pool.wait_ge(x_res_in[c % 2], (c // 2 + 1) * 16)
                pool.wait_ge(x1_scaled, c + 1)
                nc.gpsimd.tensor_tensor(vo[:, c, :], vo[:, c, :], x_res[c % 2], ALU.add).then_inc(x1_set, 1)
            with pool.Fori(0, KT // 2 - 1) as i:
                for h in range(2):
                    w_split(i * 2 + h + U_G + 2, h)

        @block.tensor
        def _(pe):
            mm = nc.tensor.matmul
            pe.wait_ge(const_set, 4)

            def v_chunk(c):
                for k in range(KT):
                    pe.wait_ge(x_lo, k + 1)
                    if k % 2 == 0:
                        pe.wait_ge(wv_lo, c * (KT // 2) + k // 2 + 1)
                    for t in range(TT):
                        if k == 0 and not isinstance(c, int):
                            pe.wait_ge((v_used_act, v_used_dve)[t % 2], (c - 1) * (TT // 2) + t // 2 + 1)
                        for n in range(MMS):
                            m = mm(ps[:, t, 0:VC], (xh, xl)[M_HALF[n]][:, k, t * P:(t + 1) * P], wv_sp[:, k, W_HALF[n], :],
                                   start=(k == 0 and n == 0), stop=(k == KT - 1 and n == MMS - 1))
                        if k == KT - 1:
                            m.then_inc(v_ready, 1)
                    if k % 2 and k < KT - 1:
                        m.then_inc(wv_used, 1)

            v_chunk(0)
            with pe.Fori(1, QUADS) as c:
                v_chunk(c)
            for used in (v_used_act, v_used_dve):
                pe.wait_ge(used, QUADS * TT // 2)

            def spread_rstd():
                for n in range(2):
                    m = mm(ps[:, 2 + n, :], ones[:], diag[:, 4 * n:4 * n + 4, :].rearrange("p t n -> p (t n)"),
                           start=True, stop=True)
                m.then_inc(rstd_spread, 1)

            for t in range(TT):
                m = nc.tensor.transpose(ps[0:HEADS, t // 4, (t % 4) * P:(t % 4 + 1) * P], fl[:, t, :], ident[:])
            m.then_inc(fl_turned, 1)
            pe.wait_ge(diag_set, 1)
            spread_rstd()

            def project(par, n, m0, m1, bank):
                for m in range(m0, m1):
                    k, e = divmod(m, MMS)
                    last = mm(ps[:, bank, :], wsp[:, par, W_HALF[e], k * P:(k + 1) * P],
                              (xh, xl)[M_HALF[e]][:, k, n * HALF:(n + 1) * HALF], start=(m == 0), stop=(m == BLOCK - 1))
                return last

            def qk_part(pr, f0, f1):
                b, m0 = divmod(f0, BLOCK)
                if m0 == 0:
                    if b % 2 == 0:
                        pe.wait_ge(w_lo, pr * 2 + b // 2 + 1)
                    if not (isinstance(pr, int) and pr == 0 and b == 0):
                        pe.wait_ge(block_lo, pr * QK_BLOCKS + b)
                last = project(b // 2, b % 2, m0, m0 + f1 - f0, PB)
                if m0 + f1 - f0 == BLOCK:
                    last.then_inc(block_ready, 1)

            for b in range(QK_BLOCKS):
                qk_part(0, b * BLOCK, (b + 1) * BLOCK)

            def logits(pr, par, j, first):
                w, nb = key_width(j)
                part = w // nb
                cols = max(part, 2 * P)
                if j == 0:
                    pe.wait_ge(block_lo, (pr + 1) * QK_BLOCKS)
                if not first:
                    pe.wait_ge(logits_set, pr * 2 * TT + 2 * j)
                for e in range(MMS):
                    for b in range(nb):
                        for r in range(2):
                            head = slice(HD * r, HD * r + HD)
                            mm(ps[:, SB + 2 * r + b, 0:cols], qk[head, par, W_HALF[e], j * P:(j + 1) * P],
                               qk[head, par, 2 + M_HALF[e], b * part:b * part + cols],
                               start=(e == 0), stop=(e == MMS - 1 and b < nb - 1), skip_group_check=True)
                for r in range(2):
                    mm(ps[:, SB + 2 * r + nb - 1, part - P:part], ident16[:], mask16[:], start=False, stop=True,
                       skip_group_check=True).then_inc(logits_ready, 1)

            def turn(pr, n):
                g, r, c = CHUNKS[n]
                if c == 0:
                    pe.wait_ge(probs_scaled, pr * 2 * TT + (2 * g + 1) * 2 + r + 1)
                if not isinstance(pr, int) or pr * NCH + n >= 2:
                    pe.wait_ge(pt_lo, pr * NCH + n - 1)
                for i in range(2):
                    for q in range(2):
                        key, query = 2 * c + i, 2 * g + q
                        src = zeros[:] if key > query else lp_at(r, query)[:, key * P:(key + 1) * P]
                        m = nc.tensor.transpose(ps[:, TB + n % 2, i * GW + q * P:i * GW + (q + 1) * P], src, ident[:])
                m.then_inc(turned, 1)

            def weigh(pr, n):
                g, r, c = CHUNKS[n]
                if c == 0:
                    if g == 0 and r == 0:
                        pe.wait_ge(vs_lo, pr * 2 + 1)
                    if not (isinstance(pr, int) and pr == 0 and g == 0 and r == 0):
                        pe.wait_ge(o_copied, pr * UNITS + 2 * g + r)
                if g == 1 and r == 0 and c == 1:
                    pe.wait_ge(vs_lo, pr * 2 + 2)
                pe.wait_ge(pt_lo, pr * NCH + n + 1)
                for i in range(2):
                    for h in range(2):
                        m = mm(ps[:, OB, 0:GW], vs[:, 2 * c + i, r, :], pt[:, n % 2, h, i, :],
                               start=(c == 0 and i == 0 and h == 0), stop=(c == g and i == 1 and h == 1))
                m.then_inc(pv_done, 1)

            def step(pr, par, first=False, last=False):
                for what, *a in step_order(first, last):
                    if what == "logits":
                        logits(pr, par, a[0], first and a[0] == 0)
                    elif what == "turn":
                        turn(pr - a[0], a[1])
                    elif what == "fill":
                        qk_part(pr + 1, a[0], a[1])
                    elif what == "weigh":
                        weigh(pr - a[0], a[1])

            step(0, 0, first=True)
            with pe.Fori(0, (PAIRS - 2) // 2) as i:
                step(i * 2 + 1, 1)
                step(i * 2 + 2, 0)
            step(PAIRS - 1, (PAIRS - 1) % 2, last=True)
            for what, *a in TAIL:
                if what == "turn":
                    turn(PAIRS - 1, a[1])
                elif what == "weigh":
                    weigh(PAIRS - 1, a[1])
                else:
                    if a[0] == 0:
                        pe.wait_ge(logits_set, PAIRS * 2 * TT)
                        pe.wait_ge(w_lo, U_Z + 1)
                    n, m0 = divmod(a[0], BLOCK)
                    m = project(0, n, m0, m0 + a[1] - a[0], n)
                    if a[1] == 2 * BLOCK:
                        m.then_inc(chunk_ready, 1)

            def whole(u, par, split=None):
                pe.wait_ge(w_lo, u + 1)
                for n in range(2):
                    for k in range(KT):
                        if split is not None and n == 0:
                            pe.wait_ge(split, k + 1)
                        last = project(par, n, k * MMS, (k + 1) * MMS, 2 * par + n)
                last.then_inc(chunk_ready, 1)

            whole(U_Z + 1, 1)
            with pe.Fori(1, KT // 2) as i:
                for h in range(2):
                    pe.wait_ge(z_mul, i * 2 + h - 1)
                    whole(i * 2 + h + U_Z, h)
            pe.wait_ge(z_mul, KT)
            whole(U_Y, 0, split=oz_lo)
            whole(U_Y + 1, 1)
            with pe.Fori(1, KT // 2) as i:
                for h in range(2):
                    pe.wait_ge(y_set, i * 2 + h - 1)
                    whole(i * 2 + h + U_Y, h)

            pe.wait_ge(sq_added, KT)
            for t in range(TT):
                m = mm(ps[:, 6, t:t + 1], sq_sum[:, t * P:(t + 1) * P], ones[:, 0:1], start=True, stop=True)
            m.then_inc(sum_ready, 1)

            def embed(c, par):
                pe.wait_ge(ple_lo, c + 1)
                for n in range(2):
                    for m in range(PK * MMS):
                        k, e = divmod(m, MMS)
                        last = mm(ps[:, 4 + 2 * par + n, :], ple_sp[:, par, W_HALF[e], k * P:(k + 1) * P],
                                  p_sp[:, M_HALF[e], k, n * HALF:(n + 1) * HALF],
                                  start=(m == 0), stop=(m == PK * MMS - 1))
                last.then_inc(ple_ready, 1)

            pe.wait_ge(p_lo, PK)
            embed(0, 0)
            pe.wait_ge(y_set, KT)
            pe.wait_ge(diag_set, 2)
            spread_rstd()
            embed(1, 1)
            whole(U_G, 0, split=x1_lo)
            pe.wait_ge(rstd_set, 2)
            whole(U_G + 1, 1)
            with pe.Fori(1, KT // 2) as i:
                for h in range(2):
                    pe.wait_ge(g_mul, i * 2 + h - 1)
                    embed(i * 2 + h, h)
                    whole(i * 2 + h + U_G, h)

        @block.scalar
        def _(act):
            A = nc.scalar.activation
            act.wait_ge(vecs_in, 4 * 16)

            def wv_split(c, par, kk, c_int):
                if kk == 0:
                    act.wait_ge(wv_in[par], (c_int // 2 + 1) * 16)
                if c_int > 0:
                    if kk < KT // 2 - 1:
                        act.wait_ge(wv_used, (c_int - 1) * (KT // 2 - 1) + kk + 1)
                    else:
                        act.wait_ge(v_ready, c_int * TT)
                A(wv_sp[:, 2 * kk:2 * kk + 2, 0, :], wv_raw[par][:, 2 * kk:2 * kk + 2, :], ACT.Copy).then_inc(wv_hi, 1)

            for k in range(KT):
                act.wait_ge(x_in[k], 16)
                A(xh[:, k, :], vo[:, k, :], ACT.Copy, scale=g_pre_sb[:, k:k + 1]).then_inc(x_hi, 1)
                if k % 2 == 0:
                    wv_split(0, 0, k // 2, 0)
            for t in range(TT):
                act.wait_ge(x_nat_in[t % 2], (t // 2 + 1) * 16)
                if t > 0:
                    act.wait_ge(squares, t)
                A(square_out, x_nat_sb[t % 2], ACT.Square, accum_out=col[:, 0, t:t + 1]).then_inc(squares, 1)

            def root(which):
                act.wait_ge(col_dve, which * 5 + 1)
                A(col[:, 3, :], col[:, 1, :], ACT.Ln).then_inc(col_act, 1)
                act.wait_ge(col_act, which * 2 + 1)
                A(col[:, 2, :], col[:, 3, :], ACT.Exp, scale=-0.5).then_inc(col_act, 1)

            root(0)
            for c in range(QUADS):
                if c + 1 < QUADS:
                    for kk in range(KT // 2 - 1):
                        wv_split(c + 1, (c + 1) % 2, kk, c + 1)
                if c == 0:
                    act.wait_ge(col_dve, 5)
                for t in range(0, TT, 2):
                    act.wait_ge(v_ready, c * TT + t + 1)
                    A(vo[:, 2 * c:2 * c + 2, t * P:(t + 1) * P], ps[:, t, 0:2 * P].rearrange("p (a n) -> p a n", a=2),
                      ACT.Copy, scale=col[:, 2, t:t + 1])
                    A(fl[:, t, 4 * c:4 * c + 4], ps[:, t, 2 * P:VC], ACT.Copy, scale=col[:, 2, t:t + 1]).then_inc(v_used_act, 1)
                if c + 1 < QUADS:
                    wv_split(c + 1, (c + 1) % 2, KT // 2 - 1, c + 1)

            def w_split(u, par, before, count):
                act.wait_ge(w_in, (u + 1) * 16)
                if before is not None:
                    act.wait_ge(before, count)
                A(wsp[:, par, 0, :], wraw[:], ACT.Copy).then_inc(w_hi, 1)

            w_split(0, 0, None, 0)
            w_split(1, 1, None, 0)
            act.wait_ge(gate_dve, 2)
            A(gate_work[2], gate_work[2], ACT.Exp).then_inc(gate_act, 1)
            act.wait_ge(gate_act, 1)
            A(gate_work[3], gate_work[2], ACT.Ln, bias=1.0).then_inc(gate_act, 1)

            def block_split(pr, par, b):
                act.wait_ge(block_scaled, pr * QK_BLOCKS + b + 1)
                A(qk[:, par, 2 * (b // 2), (b % 2) * HALF:(b % 2 + 1) * HALF], ps[:, PB, :], ACT.Copy).then_inc(block_hi, 1)

            for b in range(QK_BLOCKS):
                block_split(0, 0, b)
                if b == 1:
                    w_split(2, 0, block_ready, 2)

            def exp(pr, j, r):
                act.wait_ge(logits_set, pr * 2 * TT + 2 * j + r + 1)
                A(lp_at(r, j), lp_at(r, j), ACT.Exp, scale=-1.0, bias=nmax[:, 2 * j + r:2 * j + r + 1],
                  accum_out=rsum[:, 2 * j + r:2 * j + r + 1]).then_inc(probs_set, 1)

            def turned_hi(pr, n):
                act.wait_ge(turned, pr * NCH + n + 1)
                if not isinstance(pr, int) or pr * NCH + n >= 2:
                    act.wait_ge(pv_done, pr * NCH + n - 1)
                A(pt[:, n % 2, 0, :, :], ps[:, TB + n % 2, :].rearrange("p (i n) -> p i n", i=2), ACT.Copy).then_inc(pt_hi, 1)

            def o_copy(pr, n):
                g, r, c = CHUNKS[n]
                if c < g:
                    return
                unit = pr * UNITS + 2 * g + r
                act.wait_ge(pv_done, pr * NCH + n + 1)
                if not isinstance(pr, int) or unit >= 2:
                    act.wait_ge(o_added, unit - 1)
                head = slice(HD * r, HD * r + HD)
                A(oc[head, 0, :], ps[0:HD, OB, 0:GW], ACT.Copy)
                A(oc[head, 1, :], ps[HD:P, OB, 0:GW], ACT.Copy).then_inc(o_copied, 1)

            def v_split(pr, first):
                if not first:
                    act.wait_ge(pv_done, pr * NCH)
                for t0, t1 in ((0, 2), (2, TT)):
                    src = vo[:, bass.ds(pr, 1), t0 * P:t1 * P].rearrange("p o (s d) -> p (o s) d", d=HD)
                    wait_apart(act, act_passed)
                    A(vs[:, t0:t1, :, 0:HD].rearrange("p t r d -> p (t r) d"), src, ACT.Copy).then_inc(vs_hi, 1)

            def step(pr, par, first=False, last=False):
                for what, *a in step_order(first, last):
                    if what == "logits":
                        if a[0] == 0:
                            w_split(pr * 2 + 3, 1, block_ready, (pr + 1) * QK_BLOCKS)
                        if a[0] == 2:
                            v_split(pr, first)
                        if a[0] == 5 and not last:
                            w_split(pr * 2 + 4, 0, block_ready, (pr + 1) * QK_BLOCKS + 2)
                    elif what == "exp":
                        exp(pr, *a)
                    elif what == "turn":
                        turned_hi(pr - a[0], a[1])
                    elif what == "block":
                        block_split(pr + 1, 1 - par, a[0])
                    elif what == "weigh":
                        o_copy(pr - a[0], a[1])

            act.wait_ge(v_used_dve, QUADS * TT // 2)
            act.wait_ge(v_used_act, QUADS * TT // 2)
            step(0, 0, first=True)
            with act.Fori(0, (PAIRS - 2) // 2) as i:
                step(i * 2 + 1, 1)
                step(i * 2 + 2, 0)
            step(PAIRS - 1, (PAIRS - 1) % 2, last=True)
            for what, *a in TAIL:
                if what == "turn":
                    turned_hi(PAIRS - 1, a[1])
                elif what == "weigh":
                    o_copy(PAIRS - 1, a[1])

            def z_chunk(c, par):
                act.wait_ge(chunk_ready, c + 1)
                w_split(c + U_Z + 2, par, None, 0)
                act.wait_ge(z_scaled, c + 1)
                if later(c):
                    act.wait_ge(oz_set, c - 1)
                A(work[par], banks(2 * par), ACT.Sigmoid).then_inc(z_sig, 1)

            act.wait_ge(o_copied, PAIRS * UNITS)
            z_chunk(0, 0)
            z_chunk(1, 1)
            for k in range(PK):
                act.wait_ge(p_in[k], 16)
                A(p_sp[:, 0, k, :], cb[:, k, :], ACT.Copy).then_inc(p_hi, 1)
            with act.Fori(1, KT // 2) as i:
                for h in range(2):
                    z_chunk(i * 2 + h, h)
            for k in range(KT):
                act.wait_ge(oz_set, k + 1)
                A(xh[:, k, :], vo[:, k, :], ACT.Copy).then_inc(oz_hi, 1)

            def y_chunk(c, par):
                act.wait_ge(chunk_ready, c + KT + 1)
                y = vo[:, bass.ds(c, 1), :].rearrange("p o n -> p (o n)")
                wait_apart(act, act_passed)
                A(y, banks(2 * par), ACT.Copy).then_inc(y_set, 1)
                w_split(c + U_Y + 2, par, None, 0)
                act.wait_ge(y_set, c + 1)
                if later(c):
                    act.wait_ge(sq_added, c - 1)
                wait_apart(act, act_passed)
                A(work[par], y, ACT.Square).then_inc(sq_set, 1)

            y_chunk(0, 0)
            y_chunk(1, 1)
            with act.Fori(1, KT // 2) as i:
                for h in range(2):
                    y_chunk(i * 2 + h, h)

            root(1)

            def ple_split(c, par):
                act.wait_ge(ple_in[par], (c - par + 2) * 8)
                if later(c):
                    act.wait_ge(ple_ready, c - 1)
                A(ple_sp[:, par, 0, :], ple_raw[par], ACT.Copy).then_inc(ple_hi, 1)

            ple_split(0, 0)
            ple_split(1, 1)
            for k in range(KT):
                act.wait_ge(x1_set, k + 1)
                A(xh[:, k, :], vo[:, k, :], ACT.Copy).then_inc(x1_hi, 1)

            def g_chunk(c, par, more=True):
                act.wait_ge(chunk_ready, c + 2 * KT + 1)
                if more:
                    w_split(c + U_G + 2, par, None, 0)
                    ple_split(c + 2, par)
                if later(c):
                    act.wait_ge(out_done[par], (c - par) * 8)
                wait_apart(act, act_passed)
                A(work[par], banks(2 * par), ACT.Sigmoid,
                  bias=b_gate_sb[:, bass.ds(c, 1)]).then_inc(g_sig, 1)

            g_chunk(0, 0)
            g_chunk(1, 1)
            with act.Fori(1, KT // 2 - 1) as i:
                for h in range(2):
                    g_chunk(i * 2 + h, h)
            g_chunk(KT - 2, 0, more=False)
            g_chunk(KT - 1, 1, more=False)

        @block.vector
        def _(dve):
            tt, ts, stt = nc.vector.tensor_tensor, nc.vector.tensor_scalar, nc.vector.scalar_tensor_tensor

            def lo(out, whole, hi, done):
                tt(out, whole, f32(hi), ALU.subtract).then_inc(done, 1)

            def factors(which, sums, ready, count):
                n = which * 5
                mean, factor, work_ = (col[:, i, :] for i in (1, 2, 3))
                dve.wait_ge(ready, count)
                ts(mean, sums, 1.0 / D, EPS, ALU.mult, ALU.add).then_inc(col_dve, 1)
                dve.wait_ge(col_act, which * 2 + 2)
                tt(work_, factor, factor, ALU.mult).then_inc(col_dve, 1)
                dve.wait_ge(col_dve, n + 2)
                tt(work_, work_, mean, ALU.mult).then_inc(col_dve, 1)
                dve.wait_ge(col_dve, n + 3)
                ts(work_, work_, -0.5, 1.5, ALU.mult, ALU.add).then_inc(col_dve, 1)
                dve.wait_ge(col_dve, n + 4)
                tt(factor, factor, work_, ALU.mult).then_inc(col_dve, 1)
                dve.wait_ge(col_dve, n + 5)
                dve.wait_ge(const_set, 4)
                tt(diag, ident[:, None, :].to_broadcast([P, TT, P]), factor[:, :, None].to_broadcast([P, TT, P]),
                   ALU.mult).then_inc(diag_set, 1)

            dve.wait_ge(vecs_in, 4 * 16)

            def wv_lo_part(c, kk):
                dve.wait_ge(wv_hi, c * (KT // 2) + kk + 1)
                k = slice(2 * kk, 2 * kk + 2)
                lo(wv_sp[:, k, 1, :], wv_raw[c % 2][:, k, :], wv_sp[:, k, 0, :], wv_lo)

            for k in range(KT):
                dve.wait_ge(x_hi, k + 1)
                stt(out=xl[:, k, :], in0=vo[:, k, :], scalar=g_pre_sb[:, k:k + 1], in1=f32(xh[:, k, :]),
                    op0=ALU.mult, op1=ALU.subtract).then_inc(x_lo, 1)
                if k % 2 == 0:
                    wv_lo_part(0, k // 2)
            factors(0, col[:, 0, :], squares, TT)
            for c in range(QUADS):
                if c + 1 < QUADS:
                    for kk in range(KT // 2 - 1):
                        wv_lo_part(c + 1, kk)
                for t in range(1, TT, 2):
                    dve.wait_ge(v_ready, c * TT + t + 1)
                    ts(vo[:, 2 * c:2 * c + 2, t * P:(t + 1) * P], ps[:, t, 0:2 * P].rearrange("p (a n) -> p a n", a=2),
                       col[:, 2, t:t + 1], None, ALU.mult)
                    ts(fl[:, t, 4 * c:4 * c + 4], ps[:, t, 2 * P:VC], col[:, 2, t:t + 1], None, ALU.mult).then_inc(v_used_dve, 1)
                if c + 1 < QUADS:
                    wv_lo_part(c + 1, KT // 2 - 1)

            w0, w1, w2, w3 = gate_work
            dve.wait_ge(fl_turned, 1)
            ts(w1, ps[0:HEADS, 0:2, :].rearrange("p b n -> p (b n)"), bf[:], None, ALU.add).then_inc(gate_dve, 1)
            dve.wait_ge(gate_dve, 1)
            stt(out=w2, in0=w1, scalar=-1.0, in1=w1, op0=ALU.mult, op1=ALU.min).then_inc(gate_dve, 1)
            dve.wait_ge(rstd_spread, 1)
            nc.vector.tensor_copy(rstd_b[:], banks(2)).then_inc(rstd_set, 1)
            dve.wait_ge(gate_act, 2)
            stt(out=w2, in0=w1, scalar=0.0, in1=w3, op0=ALU.min, op1=ALU.subtract).then_inc(gate_dve, 1)
            nc.vector.memset(w0, 1.0).then_inc(gate_dve, 1)
            dve.wait_ge(gate_dve, 4)
            nc.vector.tensor_tensor_scan(w1, w0, w2, 0.0, ALU.mult, ALU.add).then_inc(gate_dve, 1)
            dve.wait_ge(gate_dve, 5)
            ts(w0, w1, -1.0 / SCALE, None, ALU.mult).then_inc(gate_dve, 1)

            def block_scale(pr, b):
                dve.wait_ge(block_ready, pr * QK_BLOCKS + b + 1)
                tt(ps[:, PB, :], ps[:, PB, :], rstd_b[:, (b % 2) * HALF:(b % 2 + 1) * HALF], ALU.mult).then_inc(block_scaled, 1)

            def block_rest(pr, par, b):
                dve.wait_ge(block_hi, pr * QK_BLOCKS + b + 1)
                half = slice((b % 2) * HALF, (b % 2 + 1) * HALF)
                lo(qk[:, par, 2 * (b // 2) + 1, half], ps[:, PB, :], qk[:, par, 2 * (b // 2), half], block_lo)

            dve.wait_ge(rstd_set, 1)
            for b in range(QK_BLOCKS):
                block_scale(0, b)
                block_rest(0, 0, b)

            def take(pr, j, r, first):
                w, nb = key_width(j)
                if j == 0 and r == 0:
                    dve.wait_ge(cb_in, (pr + 1) * 32)
                if j >= PLACES:
                    dve.wait_ge(turned, pr * NCH + chunks_until((j - PLACES) // 2, r))
                elif not first:
                    dve.wait_ge(turned, (pr - 1) * NCH + chunks_until((j + PLACES) // 2, r))
                dve.wait_ge(logits_ready, pr * 2 * TT + 2 * j + r + 1)
                wait_apart(dve, dve_passed)
                src = ps[:, SB + 2 * r:SB + 2 * r + nb, 0:w // nb]
                nc.vector.tensor_tensor_reduce(
                    out=lp_at(r, j).rearrange("p (b n) -> p b n", b=nb), in0=src,
                    in1=cb[:, r, 0:w].rearrange("p (b n) -> p b n", b=nb), scale=-SCALE, scalar=BIG,
                    op0=ALU.add, op1=ALU.min, accum_out=nmax[:, 2 * j + r:2 * j + r + 1]).then_inc(logits_set, 1)

            def scale(pr, j):
                for r in range(2):
                    n = 2 * j + r
                    dve.wait_ge(probs_set, pr * 2 * TT + n + 1)
                    nc.vector.reciprocal(rinv[:, n:n + 1], rsum[:, n:n + 1]).then_inc(sums_inverted, 1)
                for r in range(2):
                    n = 2 * j + r
                    dve.wait_ge(sums_inverted, pr * 2 * TT + n + 1)
                    ts(lp_at(r, j), lp_at(r, j), rinv[:, n:n + 1], None, ALU.mult).then_inc(probs_scaled, 1)

            def turned_lo(pr, n):
                dve.wait_ge(pt_hi, pr * NCH + n + 1)
                lo(pt[:, n % 2, 1, :, :], ps[:, TB + n % 2, :].rearrange("p (i n) -> p i n", i=2), pt[:, n % 2, 0, :, :], pt_lo)

            def step(pr, par, first=False, last=False):
                waiting = None
                for what, *a in step_order(first, last):
                    if what == "take":
                        take(pr, *a, first)
                    elif what == "scale":
                        scale(pr, a[0])
                    elif what == "turn":
                        turned_lo(pr - a[0], a[1])
                    elif what == "block":
                        block_scale(pr + 1, a[0])
                        waiting = a[0]
                        continue
                    elif what == "fill" and waiting is None:
                        continue
                    if waiting is not None:
                        block_rest(pr + 1, 1 - par, waiting)
                        waiting = None
                if waiting is not None:
                    block_rest(pr + 1, 1 - par, waiting)

            step(0, 0, first=True)
            with dve.Fori(0, (PAIRS - 2) // 2) as i:
                step(i * 2 + 1, 1)
                step(i * 2 + 2, 0)
            step(PAIRS - 1, (PAIRS - 1) % 2, last=True)
            for what, *a in TAIL:
                if what == "turn":
                    turned_lo(PAIRS - 1, a[1])

            def z_chunk(c, par):
                z = banks(2 * par)
                dve.wait_ge(chunk_ready, c + 1)
                tt(z, z, rstd_b[:], ALU.mult).then_inc(z_scaled, 1)
                dve.wait_ge(z_sig, c + 1)
                tt(work[par], z, work[par], ALU.mult).then_inc(z_mul, 1)

            z_chunk(0, 0)
            z_chunk(1, 1)
            for k in range(PK):
                dve.wait_ge(p_hi, k + 1)
                lo(p_sp[:, 1, k, :], cb[:, k, :], p_sp[:, 0, k, :], p_lo)
            with dve.Fori(1, KT // 2) as i:
                for h in range(2):
                    z_chunk(i * 2 + h, h)
            for k in range(KT):
                dve.wait_ge(oz_hi, k + 1)
                lo(xl[:, k, :], vo[:, k, :], xh[:, k, :], oz_lo)

            nc.vector.memset(sq_sum, 0.0).then_inc(sq_clear, 1)
            dve.wait_ge(sq_clear, 1)

            def y_chunk(c, par):
                dve.wait_ge(sq_set, c + 1)
                if not (isinstance(c, int) and c == 0):
                    dve.wait_ge(sq_added, c)
                tt(sq_sum, sq_sum, work[par], ALU.add).then_inc(sq_added, 1)

            y_chunk(0, 0)
            y_chunk(1, 1)
            with dve.Fori(1, KT // 2) as i:
                for h in range(2):
                    y_chunk(i * 2 + h, h)

            factors(1, ps[:, 6, 0:TT], sum_ready, 1)

            def ple_split(c, par):
                dve.wait_ge(ple_hi, c + 1)
                lo(ple_sp[:, par, 1, :], ple_raw[par], ple_sp[:, par, 0, :], ple_lo)

            ple_split(0, 0)
            ple_split(1, 1)
            dve.wait_ge(rstd_spread, 2)
            nc.vector.tensor_copy(rstd_b[:], banks(2)).then_inc(rstd_set, 1)
            dve.wait_ge(rstd_set, 2)
            for c in range(KT + 2):
                if c < KT:
                    y = vo[:, c, :]
                    stt(out=y, in0=y, scalar=g_post_sb[:, c:c + 1], in1=rstd_b[:], op0=ALU.mult,
                        op1=ALU.mult).then_inc(x1_scaled, 1)
                if c >= 2:
                    dve.wait_ge(x1_hi, c - 1)
                    lo(xl[:, c - 2, :], vo[:, c - 2, :], xh[:, c - 2, :], x1_lo)

            def g_chunk(c, par, more=True):
                if more:
                    ple_split(c + 2, par)
                dve.wait_ge(ple_ready, c + 1)
                dve.wait_ge(g_sig, c + 1)
                tt(work[par], banks(4 + 2 * par), work[par], ALU.mult).then_inc(g_mul, 1)
                dve.wait_ge(g_mul, c + 1)
                x1 = vo[:, bass.ds(c, 1), :].rearrange("p o n -> p (o n)")
                tt(work[par], work[par], x1, ALU.add).then_inc(g_add, 1)

            g_chunk(0, 0)
            g_chunk(1, 1)
            with dve.Fori(1, KT // 2 - 1) as i:
                for h in range(2):
                    g_chunk(i * 2 + h, h)
            g_chunk(KT - 2, 0, more=False)
            g_chunk(KT - 1, 1, more=False)


def chunks_of_columns(w):
    k, n = w.shape
    return np.ascontiguousarray(w.reshape(k // P, P, n // P, P).transpose(2, 1, 0, 3).reshape(n // P, P, k))


def kernel(**inputs):
    import concourse.bacc as bacc
    from concourse.bass_utils import run_bass_kernel_spmd

    a = {k: np.asarray(v) for k, v in inputs.items()}
    x, w_in = a["x"][0], a["fox_w_in"][0]
    wq, wk, wv, wz, wf = np.split(w_in, [D, 2 * D, 3 * D, 4 * D], axis=1)
    wv = np.concatenate([wv.reshape(D, QUADS, 4 * HD), wf.reshape(D, QUADS, 4)], axis=2)
    wv = np.ascontiguousarray(wv.reshape(KT, P, QUADS, VC).transpose(2, 1, 0, 3))
    q, k = chunks_of_columns(wq), chunks_of_columns(wk)
    qk = np.stack([q, k], axis=1).reshape(2 * PAIRS, P, D)
    w_all = np.concatenate([qk, chunks_of_columns(wz), chunks_of_columns(a["fox_w_out"][0]),
                            chunks_of_columns(a["ple_w_gate"][0])])
    by_tile = lambda v: np.ascontiguousarray(v.reshape(KT, P).T)
    arrays = {
        "x_nat": np.ascontiguousarray(x.reshape(TT, P, D)),
        "x_t": np.ascontiguousarray(x.T).reshape(KT, P, T),
        "wv": wv,
        "w_all": w_all,
        "w_ple": chunks_of_columns(a["ple_w_proj"][0]),
        "p_t": np.ascontiguousarray(a["p"][0, 0].T).reshape(PK, P, T),
        "f_bias": np.ascontiguousarray(a["fox_b_f"][0].reshape(HEADS, 1)),
        "g_pre": by_tile(a["ln_pre"][0]),
        "g_post": by_tile(a["ln_post"][0]),
        "b_gate": by_tile(a["ple_b_gate"][0]),
    }
    nc = bacc.Bacc("TRN2", target_bir_lowering=False, num_devices=1)
    aps = {n: nc.dram_tensor(n, v.shape, F32, kind="ExternalInput").ap() for n, v in arrays.items()}
    scratch = nc.dram_tensor("scratch", (HEADS, T), F32, kind="Internal").ap()
    out_t = nc.dram_tensor("out_t", (KT, P, T), F32, kind="ExternalOutput").ap()
    build(nc, **aps, scratch=scratch, out_t=out_t)
    r = run_bass_kernel_spmd(nc, [arrays], core_ids=[0])
    out = r.results[0]["out_t"]
    return np.ascontiguousarray(out.reshape(D, T).T).reshape(1, T, D)
```

```python
from contextlib import ExitStack

import numpy as np

import concourse.bass as bass
from concourse import mybir
from concourse.alu_op_type import AluOpType as ALU

F32 = mybir.dt.float32
F32R = mybir.dt.float32r
BF16 = mybir.dt.bfloat16
ACT = mybir.ActivationFunctionType

P = 128
D = 1024
T = 1024
KT = D // P
TT = T // P
HEADS = 16
HD = 64
PAIRS = HEADS // 2
QUADS = HEADS // 4
VC = 4 * HD + 4
RAW = 2
PLE = 256
PK = PLE // P
EPS = 1e-6
NEG = -1e30
BIG = 3e38
HALF = 512
GW = 256
GROUPS = T // GW
UNITS = 2 * GROUPS
SCALE = HD ** -0.5
MMS = 3
W_HALF = (0, 1, 0)
M_HALF = (0, 0, 1)
BLOCK = KT * MMS
HT = TT // 2
QK_BLOCKS = 4

AHEAD = 2
U0 = 2 * PAIRS + AHEAD
ZU = KT - AHEAD
JOINED = [(n, c) for n in range(2) for c in range(AHEAD)]
JOINED_AT = (4, 5, 8, 9)
V_Y = 2 * ZU
V_G = V_Y + 2 * KT


def z_item(v):
    return v + (len(JOINED) if not isinstance(v, int) or v >= ZU else 0 if v < 4 else 2)


def z_order(unit, joined):
    for v in range(ZU):
        if v:
            unit(v)
        if v in (3, 5):
            joined(v - 3)
            joined(v - 2)


CHUNKS = [(g, r, c) for g in range(GROUPS) for r in range(2) for c in range(g + 1)]
NCH = len(CHUNKS)
LAG = CHUNKS.index((GROUPS - 1, 0, 0))


def blocks_of(n):
    g, _, c = CHUNKS[n]
    return 3 if c == g else 4


def chunks_until(g, r):
    return CHUNKS.index((g, r, g)) + 1


FILL = (10, 8, 6, 12, 12, 12, 12, 24)
FILL_TO = [sum(FILL[:j + 1]) for j in range(TT)]
FIRST_TO = BLOCK


def step_order(first=False):
    def chunks_of(j):
        g = GROUPS - 1 if j < 2 else (j - 2) // 2
        back = int(j < 2)
        return [] if first and back else [(back, n) for n, (a, r, _) in enumerate(CHUNKS) if (a, r) == (g, j % 2)]

    order, filled = [], 0

    def fill(until):
        nonlocal filled
        while filled < until:
            m1 = min(until, (filled // BLOCK + 1) * BLOCK)
            order.append(("fill", filled, m1))
            filled = m1
            if filled % BLOCK == 0:
                order.append(("block", filled // BLOCK - 1))

    if first:
        fill(BLOCK // 2)
    for j in range(TT):
        mine = chunks_of(j)
        until = max(FILL_TO[j], FIRST_TO) if first else FILL_TO[j]
        following = chunks_of(j + 1) if j % 2 == 0 else []
        order.append(("logits", j))
        start, parts = filled, len(mine) + 1
        share = lambda q: start + max(0, until - start) * q // parts
        order.append(("take", j, 0))
        rest = [("scale", int(j == 0), (j - 1) % TT, 1)] if j % 2 == 0 and (j or not first) else []
        if len(mine) < 2:
            order += rest
        if j % 2 == 0 and mine:
            order.append(("turn", *mine[0]))
            fill(share(1))
        if len(mine) >= 2:
            order += rest
        order += [("take", j, 1), ("exp", j, 0)]
        if j % 2 and not mine:
            order += [("scale", 0, j - 1, r) for r in range(2)]
        for q, chunk in enumerate(mine):
            for ahead in (mine + following)[q + 1:q + 2]:
                order.append(("turn", *ahead))
            if q == 0:
                order.append(("exp", j, 1))
                if j % 2:
                    order += [("scale", 0, j - 1, r) for r in range(2)]
            if j % 2 and q == len(mine) - 1:
                order.append(("scale", 0, j, 0))
            fill(share(q + 2))
            order.append(("weigh", *chunk))
        if not mine:
            order.append(("exp", j, 1))
            if j % 2:
                order.append(("scale", 0, j, 0))
        fill(until)
    return order


TAIL_FILL = (0, 6, 12, 16, 20, 24, 30, 36, 42, 48)
TAIL = [("fill", *TAIL_FILL[:2]), ("turn", 0, LAG), ("scale", 0, TT - 1, 1)] + [
    x for n in range(LAG, NCH) for x in
    ([("turn", 0, n + 1)] if n + 1 < NCH else []) +
    [("fill", TAIL_FILL[n - LAG + 1], TAIL_FILL[n - LAG + 2]), ("weigh", 0, n)]]
UNIT_0_DONE = LAG + 3


def key_width(j):
    w = (j + 1) * P
    return w, (1 if w <= HALF else 2)


PLACES = 4
PLACE_W = [(TT - PLACES + 1 + s) * P for s in range(PLACES)]
PLACE_AT = [sum(PLACE_W[:s]) for s in range(PLACES)]
HEAD_W = sum(PLACE_W)


def build(nc, x_t, wv, w_all, w_ple, p_t, f_bias, vectors, scratch, out_t):
    with ExitStack() as ctx:
        def sb(name, shape, dt):
            return ctx.enter_context(nc.sbuf_tensor(name, shape, dt))

        def sem(name):
            return ctx.enter_context(nc.semaphore(name))

        xh = sb("xh", [P, KT, T], F32R)
        xl = sb("xl", [P, KT, T], F32R)
        qk = sb("qk", [P, 2, 4, T], F32R)
        vs = sb("vs", [P, TT, 2, P], F32R)
        pt = sb("pt", [P, 1 + 2 * 2 * 4, P], F32R)
        wraw = sb("wraw", [P, 2, KT * P], F32)
        wsp = sb("wsp", [P, 2, 2, KT * P], F32R)
        vo = sb("vo", [P, PAIRS, T], F32)
        lp = sb("lp", [P, 2 * HEAD_W], F32)
        cb = sb("cb", [P, 2, T], F32)
        ident = sb("ident", [P, P], F32)
        ident16 = sb("ident16", [P, P], BF16)
        mask16 = sb("mask16", [P, P], BF16)
        ones = sb("ones", [P, P], F32)
        zeros = sb("zeros", [P, P], F32)
        fl = sb("fl", [P, TT, HEADS], F32)
        vecs = sb("vecs", [P, 3, KT], F32)
        bf = sb("bf", [HEADS, 1], F32)
        col = sb("col", [P, 3, TT], F32)
        nmax = sb("nmax", [P, 2 * TT], F32)
        rsum = sb("rsum", [P, 2 * TT], F32)
        rinv = sb("rinv", [P, 2 * TT], F32)
        oc = sb("oc", [P, 2, GW], F32)
        ps = ctx.enter_context(nc.psum_tensor("ps", [P, 8, HALF], F32))
        SB, TB, OB, PB = 0, 4, 6, 7
        BLOCK_BANK, FB = (0, 1, 4, 5), 2

        g_pre_sb, g_post_sb, b_gate_sb = (vecs[:, i, :] for i in range(3))
        wv_raw = [lp[:, i * KT * VC:(i + 1) * KT * VC].rearrange("p (k n) -> p k n", k=KT) for i in range(2)]
        x_sum = [cb[:, 0, :], cb[:, 1, :], lp[:, 2 * KT * VC:2 * KT * VC + T]]
        square = [cb[:, 1, :], wraw[:, 1, :]]
        wv_sp = qk[:].rearrange("p a b t -> p (a b t)")[:, 0:KT * 2 * VC].rearrange("p (k h n) -> p k h n", k=KT, h=2)
        diag = lp[:, 2 * HEAD_W - TT * P:].rearrange("p (t n) -> p t n", t=TT)
        rstd_x = lp[:, 2 * HEAD_W - T:]
        gate_work = [lp[0:HEADS, i * T:(i + 1) * T] for i in range(4)]
        work = [lp[:, i * HALF:(i + 1) * HALF] for i in range(2)]
        x_res = [lp[:, (2 + i) * HALF:(3 + i) * HALF] for i in range(4)]
        ple_raw = [lp[:, 6 * HALF + i * PLE:6 * HALF + (i + 1) * PLE] for i in range(2)]
        rstd_y = lp[:, 7 * HALF:7 * HALF + T]
        ple_sp = vs[:].rearrange("p a b n -> p (a b n)")[:, 0:4 * PK * P].rearrange("p (i h n) -> p i h n", i=2, h=2)
        p_sp = qk[:, 1, :, :].rearrange("p (h k) t -> p h k t", h=2)
        sq_sum = cb[:, 0, :]

        def half(n):
            return slice(n * HALF, (n + 1) * HALF)

        def o_tile(c, n):
            return vo[:, bass.ds(c, 1), half(n)].rearrange("p o n -> p (o n)")

        def f32(ap):
            return ap.bitcast(F32)

        def banks(bank, n=2):
            return ps[:, bank:bank + n, :].rearrange("p b n -> p (b n)")

        def lp_at(r, j):
            at = r * HEAD_W + PLACE_AT[j % PLACES]
            return lp[:, at:at + (j + 1) * P]

        def turned_at(n, h):
            at = 1 + n % 2 * 8 + h * 4
            return pt[:, at:at + blocks_of(n), :].rearrange("p b n -> p (b n)")

        def turned_key(n, h, i):
            at = 1 + n % 2 * 8 + h * 4 + 2 * i
            return pt[:, 0:at + 1:at, :] if i == 1 and blocks_of(n) == 3 else pt[:, at:at + 2, :]

        x_in = [sem(f"x_in{k}") for k in range(KT)]
        wv0_in = [sem(f"wv0_in{i}") for i in range(KT // 2)]
        w_in = [sem(f"w_in{i}") for i in range(2)]
        wv_in = [sem(f"wv_in{i}") for i in range(2)]
        x_res_in = [sem(f"x_res_in{i}") for i in range(4)]
        ple_in = [sem(f"ple_in{i}") for i in range(2)]
        out_done = [sem(f"out_done{i}") for i in range(2)]
        p_in = [sem(f"p_in{i}") for i in range(PK)]
        (x0_in, x0_hi, x0_lo) = map(sem, ("x0_in", "x0_hi", "x0_lo"))
        (vecs_in, bf_in, cb_in, gates_out) = map(sem, ("vecs_in", "bf_in", "cb_in", "gates_out"))
        (zeros_set, zero_block, const_set, x_hi, x_lo, wv_hi, wv_lo, tiles_used, v_ready, v_used_act, v_used_dve) = map(sem, (
            "zeros_set", "zero_block", "const_set", "x_hi", "x_lo", "wv_hi", "wv_lo", "tiles_used", "v_ready", "v_used_act", "v_used_dve"))
        (squares, squares_added, raw_scaled, col_act, col_dve, diag_set, rstd_spread, rstd_set, fl_turned, gate_act, gate_dve) = map(sem, (
            "squares", "squares_added", "raw_scaled", "col_act", "col_dve", "diag_set", "rstd_spread", "rstd_set", "fl_turned", "gate_act", "gate_dve"))
        (w_hi, w_lo, block_ready, block_hi, block_lo, x_summed, x_scaled) = map(sem, (
            "w_hi", "w_lo", "block_ready", "block_hi", "block_lo", "x_summed", "x_scaled"))
        (logits_ready, logits_set, probs_set, sums_inverted, probs_scaled) = map(sem, (
            "logits_ready", "logits_set", "probs_set", "sums_inverted", "probs_scaled"))
        (turned, pt_hi, pt_lo, pv_done, o_copied, o_added, vs_hi, vs_lo) = map(sem, (
            "turned", "pt_hi", "pt_lo", "pv_done", "o_copied", "o_added", "vs_hi", "vs_lo"))
        (unit_ready, z_joined, z_sig, z_mul, oz_set, oz_hi, oz_lo, p_hi, p_lo) = map(sem, (
            "unit_ready", "z_joined", "z_sig", "z_mul", "oz_set", "oz_hi", "oz_lo", "p_hi", "p_lo"))
        (y_set, sq_set, sq_added, sum_ready, x1_scaled, x1_set, x1_hi, x1_lo) = map(sem, (
            "y_set", "sq_set", "sq_added", "sum_ready", "x1_scaled", "x1_set", "x1_hi", "x1_lo"))
        (ple_hi, ple_lo, ple_ready, g_sig, g_mul, g_add) = map(sem, (
            "ple_hi", "ple_lo", "ple_ready", "g_sig", "g_mul", "g_add"))
        act_passed, dve_passed, pool_passed = map(sem, ("act_passed", "dve_passed", "pool_passed"))
        block = ctx.enter_context(nc.Block())

        def later(c, n=0):
            return n > 0 or not (isinstance(c, int) and c < 2)

        def units(eng, unit, c0=0, c1=KT):
            with eng.Fori(c0 // 2, c1 // 2) as i:
                for par in range(2):
                    unit(i * 2 + par, par)

        def wait_apart(eng, passed):
            eng.sem_inc(passed, 1)

        @block.sync
        def _(sp):
            def load_w(u, par, back=0):
                if not isinstance(u, int) or u >= 2:
                    sp.wait_ge(w_lo, u - 1)
                sp.dma_start(wraw[:, par, :], w_all[bass.ds(u - back, 1), :, :].rearrange("o p n -> p (o n)")).then_inc(w_in[par], 16)

            def load_gates(pr):
                for r in range(2):
                    sp.dma_start(cb[:, r, :], scratch[bass.ds(pr * 2 + r, 1), :].to_broadcast([P, T])).then_inc(cb_in, 16)

            def load_wv0(kk):
                k = slice(2 * kk, 2 * kk + 2)
                sp.dma_start(wv_raw[0][:, k, :], wv[0, :, k, :]).then_inc(wv0_in[kk], 16)

            sp.dma_start(vecs[:], vectors).then_inc(vecs_in, 16)
            sp.dma_start(vo[:, 0, half(0)], x_t[0, :, half(0)]).then_inc(x0_in, 16)
            load_wv0(0)
            sp.dma_start(vo[:, 0, half(1)], x_t[0, :, half(1)]).then_inc(x_in[0], 16)
            for k in range(1, KT):
                sp.dma_start(vo[:, k, :], x_t[k, :, :]).then_inc(x_in[k], 16)
                if k % 2 == 0:
                    load_wv0(k // 2)
            sp.dma_start(bf[:], f_bias).then_inc(bf_in, 16)
            sp.dma_start(wv_raw[1], wv[1, :, :, :]).then_inc(wv_in[1], 16)
            load_w(0, 0)
            for c in range(2, QUADS):
                sp.wait_ge(wv_lo, (c - 1) * KT // 2)
                sp.dma_start(wv_raw[c % 2], wv[c, :, :, :]).then_inc(wv_in[c % 2], 16)
            sp.wait_ge(squares_added, KT - 1)
            load_w(1, 1)
            load_w(2, 0)
            sp.wait_ge(gate_dve, 6)
            sp.dma_start(scratch, gate_work[0]).then_inc(gates_out, 16)
            sp.wait_ge(gates_out, 16)
            sp.wait_ge(x_lo, 2 * KT)
            load_gates(0)
            load_w(3, 1)
            with sp.Fori(0, PAIRS - 1) as pr:
                load_w(pr * 2 + 4, 0)
                load_w(pr * 2 + 5, 1)
                sp.wait_ge(logits_set, (pr + 1) * 2 * TT)
                load_gates(pr + 1)
            load_w(U0, 0)
            load_w(U0 + 1, 1)
            sp.wait_ge(logits_set, PAIRS * 2 * TT)
            for k in range(PK):
                sp.dma_start(cb[:, k, :], p_t[k, :, :]).then_inc(p_in[k], 16)

            def load_units(v0, v1, back):
                units(sp, lambda v, par: load_w(v + U0, par, back), v0, v1)

            def load_ple(c, n, par):
                if later(c, n):
                    sp.wait_ge(ple_lo, n * KT + c - 1)
                sp.dma_start(ple_raw[par], w_ple[bass.ds(c, 1), :, :].rearrange("o p n -> p (o n)")).then_inc(ple_in[par], 16)

            def load_x(e):
                if e >= 4:
                    sp.wait_ge(x1_set, e - 3)
                sp.dma_start(x_res[e % 4], x_t[e % KT, :, half(e // KT)]).then_inc(x_res_in[e % 4], 16)

            load_units(2, ZU, 0)
            load_units(ZU, V_Y + KT, ZU)
            sp.wait_ge(z_mul, JOINED_AT[-1] + 1)
            for e in range(4):
                load_x(e)
            load_ple(0, 0, 0)
            load_ple(1, 0, 1)
            load_units(V_Y + KT, V_G, ZU + KT)
            for i in range(4):
                load_w(U0 + V_G + i, i % 2, ZU + KT)
                for e in (2 * i + 4, 2 * i + 5):
                    load_x(e)
                if i < 2:
                    load_ple(i + 2, 0, i)

            def store(c, n, par):
                sp.wait_ge(g_add, n * KT + c + 1)
                sp.dma_start(out_t[bass.ds(c, 1), :, half(n)].rearrange("o p n -> p (o n)"), work[par]).then_inc(out_done[par], 16)

            def g_unit(c, n, par):
                load_w(c + (U0 + V_G + n * KT + 4), par, ZU + (n + 1) * KT)
                load_ple(c + 4, n, par)
                store(c, n, par)

            units(sp, lambda c, par: g_unit(c, 0, par), 0, KT - 4)
            for c in range(KT - 4, KT):
                load_w(c + U0 + V_G + 4, c % 2, ZU + 2 * KT)
                if c < KT - 2:
                    for e in (2 * c + 4, 2 * c + 5):
                        load_x(e)
                load_ple(c + 4 - KT, 1, c % 2)
                store(c, 0, c % 2)
            units(sp, lambda c, par: g_unit(c, 1, par), 0, KT - 4)
            units(sp, lambda c, par: store(c, 1, par), KT - 4)
            for par in range(2):
                sp.wait_ge(out_done[par], KT * 16)

        @block.gpsimd
        def _(pool):
            nc.gpsimd.memset(zeros[:], 0.0).then_inc(zeros_set, 1)
            nc.gpsimd.memset(ones[:], 1.0).then_inc(const_set, 1)
            pool.wait_ge(zeros_set, 1)
            nc.gpsimd.affine_select(out=ident[:], in_=zeros[:], compare_op=ALU.not_equal, fill=1.0, base=0,
                                    pattern=[[-1, P]], channel_multiplier=1).then_inc(const_set, 1)
            nc.gpsimd.affine_select(out=mask16[:], in_=zeros[:], compare_op=ALU.is_ge, fill=NEG, base=0,
                                    pattern=[[-1, P]], channel_multiplier=1).then_inc(const_set, 1)
            pool.wait_ge(const_set, 2)
            nc.gpsimd.tensor_copy(ident16[:], ident[:]).then_inc(const_set, 1)

            for k in range(1, KT):
                pool.wait_ge(squares, k + 1)
                if k >= 2:
                    pool.wait_ge(squares_added, k - 1)
                nc.gpsimd.tensor_tensor(sq_sum, sq_sum, square[k % 2], ALU.add).then_inc(squares_added, 1)

            def w_split(u, par):
                pool.wait_ge(w_hi, u + 1)
                nc.gpsimd.tensor_tensor(wsp[:, par, 1, :], wraw[:, par, :], f32(wsp[:, par, 0, :]), ALU.subtract).then_inc(w_lo, 1)

            w_split(0, 0)
            pool.wait_ge(sum_ready, 1)
            for k in range(KT):
                if k < KT - 1:
                    pool.wait_ge(tiles_used, (QUADS - 1) * (KT - 1) + k + 1)
                else:
                    pool.wait_ge(v_ready, QUADS * TT)
                if k >= 3:
                    pool.wait_ge(x_lo, KT + k - 2)
                nc.gpsimd.tensor_tensor(x_sum[k % 3], f32(xh[:, k, :]), f32(xl[:, k, :]), ALU.add).then_inc(x_summed, 1)
            for u in range(1, 3):
                w_split(u, u % 2)

            def v_split(pr, first):
                if not first:
                    pool.wait_ge(o_added, pr * UNITS)
                for i, (t0, t1) in enumerate(((0, 2), (2, TT))):
                    pool.wait_ge(vs_hi, pr * 2 + i + 1)
                    src = vo[:, bass.ds(pr, 1), t0 * P:t1 * P].rearrange("p o (s d) -> p (o s) d", d=HD)
                    v = vs[:, t0:t1, :, :].rearrange("p t r d -> p (t r) d")
                    wait_apart(pool, pool_passed)
                    nc.gpsimd.tensor_tensor(v[:, :, HD:P], src, f32(v[:, :, 0:HD]), ALU.subtract).then_inc(vs_lo, 1)

            def o_add(pr, n, split):
                g, r, c = CHUNKS[n]
                if c < g:
                    return
                head = slice(HD * r, HD * r + HD)
                pool.wait_ge(*split)
                pool.wait_ge(o_copied, pr * UNITS + 2 * g + r + 1)
                dst = vo[head, bass.ds(pr, 1), g * GW:(g + 1) * GW].rearrange("p o n -> p (o n)")
                wait_apart(pool, pool_passed)
                nc.gpsimd.tensor_tensor(dst, oc[head, 0, :], oc[head, 1, :], ALU.add).then_inc(o_added, 1)

            def step(pr, first=False):
                split = None if first else (w_lo, pr * 2 + 3)
                for what, *a in step_order(first):
                    if what == "logits":
                        if a[0] == 2:
                            v_split(pr, first)
                            split = vs_lo, pr * 2 + 2
                        if a[0] == 3:
                            pool.wait_ge(o_added, pr * UNITS + 1)
                            w_split(pr * 2 + 3, 1)
                            split = w_lo, pr * 2 + 4
                        if a[0] == 5:
                            pool.wait_ge(o_added, pr * UNITS + 3)
                            w_split(pr * 2 + 4, 0)
                            split = w_lo, pr * 2 + 5
                    elif what == "weigh":
                        o_add(pr - a[0], a[1], split)

            step(0, first=True)
            with pool.Fori(1, PAIRS) as pr:
                step(pr)
            pool.wait_ge(o_added, PAIRS * UNITS - 2)
            w_split(U0 + 1, 1)
            split = w_lo, U0 + 2
            for what, *a in TAIL:
                if what == "weigh":
                    o_add(PAIRS - 1, a[1], split)
                    if a[1] == UNIT_0_DONE:
                        pool.wait_ge(o_added, PAIRS * UNITS - 1)
                        w_split(U0 + 2, 0)
                        split = w_lo, U0 + 3

            pool.wait_ge(o_added, PAIRS * UNITS)
            w_split(U0 + 3, 1)

            def gate_o(c, n, par, item):
                pool.wait_ge(z_mul, item + 1)
                wait_apart(pool, pool_passed)
                nc.gpsimd.tensor_tensor(o_tile(c, n), o_tile(c, n), work[par], ALU.mult).then_inc(oz_set, 1)


            def z_unit(c, par, n):
                v = c + (n * ZU - AHEAD)
                if not (isinstance(v, int) and v == 1):
                    w_split(v + (U0 + 2), par)
                gate_o(c, n, par, z_item(v))

            gate_o(AHEAD, 0, 0, 0)
            z_order(lambda v: z_unit(v + AHEAD, v % 2, 0),
                    lambda i: gate_o(JOINED[i][1], JOINED[i][0], i % 2, JOINED_AT[i]))
            units(pool, lambda c, par: z_unit(c, par, 1), AHEAD)

            def add_x(n, i):
                for h in range(2):
                    pool.wait_ge(x_res_in[(2 * i + h) % 4], (n * KT + 2 * i + h) // 4 * 16 + 16)
                    pool.wait_ge(x1_scaled, n * KT + 2 * i + h + 1)
                    y = vo[:, 2 * i + h, half(n)]
                    nc.gpsimd.tensor_tensor(y, y, x_res[(2 * i + h) % 4], ALU.add).then_inc(x1_set, 1)

            def plain(first):
                return lambda c, par: w_split(c + (U0 + first + 2), par)

            units(pool, plain(V_Y))
            for n in range(2):
                first = V_Y + KT + n * KT
                units(pool, plain(first), 0, KT // 2)
                for i in range(KT // 2):
                    add_x(n, i)
                    w_split(U0 + first + KT // 2 + i + 2, i % 2)
            units(pool, plain(V_G + KT), 0, KT - 2)

        @block.tensor
        def _(pe):
            mm = nc.tensor.matmul
            pe.wait_ge(const_set, 4)

            def v_chunk(c):
                for k in range(KT):
                    if k == 0 and c == 0:
                        pe.wait_ge(x0_lo, 1)
                    else:
                        pe.wait_ge(x_lo, k + 1)
                    if k % 2 == 0:
                        pe.wait_ge(wv_lo, c * (KT // 2) + k // 2 + 1)
                    for t in range(TT):
                        if k == 0 and c == 0 and t == HT:
                            pe.wait_ge(x_lo, 1)
                        if k == 0 and c > 0:
                            pe.wait_ge((v_used_act, v_used_dve)[t % 2], (c - 1) * (TT // 2) + t // 2 + 1)
                        for n in range(MMS):
                            m = mm(ps[:, t, 0:VC], (xh, xl)[M_HALF[n]][:, k, t * P:(t + 1) * P], wv_sp[:, k, W_HALF[n], :],
                                   start=(k == 0 and n == 0), stop=(k == KT - 1 and n == MMS - 1))
                        if k == KT - 1:
                            m.then_inc(v_ready, 1)
                    if k < KT - 1:
                        m.then_inc(tiles_used, 1)

            def spread_rstd(bank, halves):
                for n in range(halves):
                    m = mm(ps[:, bank + n, :], ones[:], diag[:, 4 * n:4 * n + 4, :].rearrange("p t n -> p (t n)"),
                           start=True, stop=True)
                m.then_inc(rstd_spread, 1)

            def sum_squares(bank, at, t0, t1):
                for t in range(t0, t1):
                    m = mm(ps[:, bank, at + t - t0:at + t - t0 + 1], sq_sum[:, t * P:(t + 1) * P], ones[:, 0:1],
                           start=True, stop=True)
                m.then_inc(sum_ready, 1)

            v_chunk(0)
            v_chunk(1)
            pe.wait_ge(squares_added, KT - 1)
            pe.wait_ge(v_used_act, TT // 2 + 1)
            sum_squares(0, 0, 0, TT)
            pe.wait_ge(col_dve, 1)
            v_chunk(2)
            pe.wait_ge(diag_set, 1)
            for used in (v_used_act, v_used_dve):
                pe.wait_ge(used, 2 * (TT // 2) + 2)
            spread_rstd(2, 2)
            pe.wait_ge(rstd_set, 2)
            v_chunk(3)

            def project(par, n, m0, m1, bank):
                for m in range(m0, m1):
                    k, e = divmod(m, MMS)
                    last = mm(ps[:, bank, :], wsp[:, par, W_HALF[e], k * P:(k + 1) * P],
                              (xh, xl)[M_HALF[e]][:, k, n * HALF:(n + 1) * HALF], start=(m == 0), stop=(m == BLOCK - 1))
                return last

            def qk_part(pr, f0, f1):
                b, m0 = divmod(f0, BLOCK)
                if m0 == 0:
                    if b % 2 == 0:
                        pe.wait_ge(w_lo, pr * 2 + b // 2 + 1)
                    if not (isinstance(pr, int) and pr == 1 and b == 0):
                        pe.wait_ge(block_lo, pr * QK_BLOCKS + b)
                last = project(b // 2, b % 2, m0, m0 + f1 - f0, PB)
                if m0 + f1 - f0 == BLOCK:
                    last.then_inc(block_ready, 1)

            for b in range(QK_BLOCKS):
                if b % 2 == 0:
                    pe.wait_ge(w_lo, b // 2 + 1)
                pe.wait_ge((v_used_act, v_used_dve)[b % 2], (QUADS - 1) * (TT // 2) + BLOCK_BANK[b] // 2 + 1)
                for k in range(KT):
                    if b == 0:
                        pe.wait_ge(x_lo, KT + k + 1)
                    last = project(b // 2, b % 2, k * MMS, (k + 1) * MMS, BLOCK_BANK[b])
                last.then_inc(block_ready, 1)
                if b == 0:
                    for used in (v_used_act, v_used_dve):
                        pe.wait_ge(used, QUADS * TT // 2)
                    pe.wait_ge(raw_scaled, 3)
                    for t in range(TT):
                        m = nc.tensor.transpose(ps[0:HEADS, FB + t // 4, (t % 4) * P:(t % 4 + 1) * P], fl[:, t, :], ident[:])
                    m.then_inc(fl_turned, 1)

            pe.wait_ge(zero_block, 1)

            def logits(pr, par, j, first):
                w, nb = key_width(j)
                part = w // nb
                cols = max(part, 2 * P)
                if j == 0:
                    pe.wait_ge(block_lo, (pr + 1) * QK_BLOCKS - 1)
                if j == TT // 2:
                    pe.wait_ge(block_lo, (pr + 1) * QK_BLOCKS)
                if not first:
                    pe.wait_ge(logits_set, pr * 2 * TT + 2 * j)
                for e in range(MMS):
                    for b in range(nb):
                        for r in range(2):
                            head = slice(HD * r, HD * r + HD)
                            mm(ps[:, SB + 2 * r + b, 0:cols], qk[head, par, W_HALF[e], j * P:(j + 1) * P],
                               qk[head, par, 2 + M_HALF[e], b * part:b * part + cols],
                               start=(e == 0), stop=(e == MMS - 1 and b < nb - 1), skip_group_check=True)
                for r in range(2):
                    mm(ps[:, SB + 2 * r + nb - 1, part - P:part], ident16[:], mask16[:], start=False, stop=True,
                       skip_group_check=True).then_inc(logits_ready, 1)

            def turn(pr, n):
                g, r, c = CHUNKS[n]
                if c == 0:
                    pe.wait_ge(probs_scaled, pr * 2 * TT + (2 * g + 1) * 2 + r + 1)
                if not isinstance(pr, int) or pr * NCH + n >= 2:
                    pe.wait_ge(pt_lo, pr * NCH + n - 1)
                blocks = [(2 * c + i, 2 * g + q) for i in range(2) for q in range(2) if 2 * c + i <= 2 * g + q]
                for at, (key, query) in enumerate(blocks):
                    src = lp_at(r, query)[:, key * P:(key + 1) * P]
                    m = nc.tensor.transpose(ps[:, TB + n % 2, at * P:(at + 1) * P], src, ident[:])
                m.then_inc(turned, 1)

            def weigh(pr, n):
                g, r, c = CHUNKS[n]
                if c == 0:
                    if g == 0 and r == 0:
                        pe.wait_ge(vs_lo, pr * 2 + 1)
                    if not (isinstance(pr, int) and pr == 0 and g == 0 and r == 0):
                        pe.wait_ge(o_copied, pr * UNITS + 2 * g + r)
                if g == 1 and r == 0 and c == 1:
                    pe.wait_ge(vs_lo, pr * 2 + 2)
                pe.wait_ge(pt_lo, pr * NCH + n + 1)
                for i in range(2):
                    for h in range(2):
                        m = mm(ps[:, OB, 0:GW], vs[:, 2 * c + i, r, :], turned_key(n, h, i),
                               start=(c == 0 and i == 0 and h == 0), stop=(c == g and i == 1 and h == 1))
                m.then_inc(pv_done, 1)

            def step(pr, par, first=False):
                for what, *a in step_order(first):
                    if what == "logits":
                        logits(pr, par, a[0], first and a[0] == 0)
                    elif what == "turn":
                        turn(pr - a[0], a[1])
                    elif what == "fill":
                        qk_part(pr + 1, a[0], a[1])
                    elif what == "weigh":
                        weigh(pr - a[0], a[1])

            step(0, 0, first=True)
            with pe.Fori(0, (PAIRS - 2) // 2) as i:
                step(i * 2 + 1, 1)
                step(i * 2 + 2, 0)
            step(PAIRS - 1, (PAIRS - 1) % 2)
            for what, *a in TAIL:
                if what == "turn":
                    turn(PAIRS - 1, a[1])
                elif what == "weigh":
                    weigh(PAIRS - 1, a[1])
                elif what == "fill":
                    if a[0] == 0:
                        pe.wait_ge(logits_set, PAIRS * 2 * TT)
                    v, m0 = divmod(a[0], BLOCK)
                    if m0 == 0:
                        pe.wait_ge(w_lo, U0 + v + 1)
                    m = project(v, 0, m0, m0 + a[1] - a[0], v)
                    if m0 + a[1] - a[0] == BLOCK:
                        m.then_inc(unit_ready, 1)

            def unit(v, par, n, split=None):
                pe.wait_ge(w_lo, v + U0 + 1)
                for k in range(KT):
                    if split is not None:
                        pe.wait_ge(split, n * KT + k + 1)
                    last = project(par, n, k * MMS, (k + 1) * MMS, par)
                last.then_inc(unit_ready, 1)

            def z_unit(v, par, n):
                pe.wait_ge(z_mul, z_item(v - 2) + 1)
                unit(v, par, n)

            for v in range(2, ZU):
                z_unit(v, v % 2, 0)
            for v in range(ZU, ZU + 2):
                z_unit(v, v % 2, 1)
            units(pe, lambda v, par: z_unit(v, par, 1), ZU + 2, V_Y)

            def y_unit(c, par, n):
                if later(c, n):
                    pe.wait_ge(y_set, c + (n * KT - 1))
                else:
                    pe.wait_ge(z_mul, len(JOINED) + 2 * ZU - 1 + c)
                first = isinstance(c, int) and c == 0
                unit(c + (V_Y + n * KT), par, n, split=oz_lo if first else None)

            def embed(c, par, n):
                pe.wait_ge(ple_lo, c + (n * KT + 1))
                if later(c, n):
                    pe.wait_ge(g_mul, c + (n * KT - 1))
                for m in range(PK * MMS):
                    k, e = divmod(m, MMS)
                    last = mm(ps[:, 2 + par, :], ple_sp[:, par, W_HALF[e], k * P:(k + 1) * P],
                              p_sp[:, M_HALF[e], k, half(n)], start=(m == 0), stop=(m == PK * MMS - 1))
                last.then_inc(ple_ready, 1)

            def g_unit(c, par, n):
                embed(c, par, n)
                if not later(c, n):
                    pe.wait_ge(y_set, 2 * KT - 1 + c)
                first = isinstance(c, int) and c == 0
                unit(c + (V_G + n * KT), par, n, split=x1_lo if first else None)

            def half_units(unit_, n, norm=None):
                peeled = 2 if norm is None else 4
                for c in range(peeled):
                    unit_(c, c % 2, n)
                    if norm is not None and c == 0:
                        pe.wait_ge(sq_added, (norm + 1) * KT)
                        sum_squares(6, norm * HT, norm * HT, (norm + 1) * HT)
                    if norm is not None and c == 2:
                        pe.wait_ge(diag_set, norm + 2)
                        spread_rstd(7, 1)
                units(pe, lambda c, par: unit_(c, par, n), peeled)

            half_units(y_unit, 0)
            half_units(y_unit, 1, norm=0)
            pe.wait_ge(p_lo, PK)
            half_units(g_unit, 0, norm=1)
            half_units(g_unit, 1)

        @block.scalar
        def _(act):
            A = nc.scalar.activation
            act.wait_ge(zeros_set, 1)
            A(pt[:, 0, :], zeros[:], ACT.Copy).then_inc(zero_block, 1)
            act.wait_ge(vecs_in, 16)

            def wv_split(c, par, kk, c_int):
                if c_int == 0:
                    act.wait_ge(wv0_in[kk], 16)
                elif kk == 0:
                    act.wait_ge(wv_in[par], (c_int + 1) // 2 * 16)
                if c_int > 0:
                    if kk < KT // 2 - 1:
                        act.wait_ge(tiles_used, (c_int - 1) * (KT - 1) + 2 * kk + 2)
                    else:
                        act.wait_ge(v_ready, c_int * TT)
                A(wv_sp[:, 2 * kk:2 * kk + 2, 0, :], wv_raw[par][:, 2 * kk:2 * kk + 2, :], ACT.Copy).then_inc(wv_hi, 1)

            act.wait_ge(x0_in, 16)
            A(xh[:, 0, half(0)], vo[:, 0, half(0)], ACT.Copy, scale=g_pre_sb[:, 0:1]).then_inc(x0_hi, 1)
            wv_split(0, 0, 0, 0)
            for k in range(KT):
                tokens = slice(0 if k else HALF, T)
                act.wait_ge(x_in[k], 16)
                A(xh[:, k, tokens], vo[:, k, tokens], ACT.Copy, scale=g_pre_sb[:, k:k + 1]).then_inc(x_hi, 1)
                if k and k % 2 == 0:
                    wv_split(0, 0, k // 2, 0)
                if k >= 3:
                    act.wait_ge(squares_added, k - 2)
                A(square[k % 2] if k else sq_sum, vo[:, k, :], ACT.Square).then_inc(squares, 1)
            def root(which, tiles):
                act.wait_ge(col_dve, which * 5 + 1)
                A(col[:, 2, 0:tiles], col[:, 0, 0:tiles], ACT.Ln).then_inc(col_act, 1)
                act.wait_ge(col_act, which * 2 + 1)
                A(col[:, 1, 0:tiles], col[:, 2, 0:tiles], ACT.Exp, scale=-0.5).then_inc(col_act, 1)

            def x_split(k):
                act.wait_ge(x_scaled, k + 1)
                A(xh[:, k, :], x_sum[k % 3], ACT.Copy).then_inc(x_hi, 1)

            def w_split(u, par, before, count):
                act.wait_ge(w_in[par], (u - par + 2) * 8)
                if before is not None:
                    act.wait_ge(before, count)
                A(wsp[:, par, 0, :], wraw[:, par, :], ACT.Copy).then_inc(w_hi, 1)

            for c in range(QUADS):
                if c == RAW:
                    root(0, TT)
                if c + 1 < QUADS:
                    for kk in range(KT // 2 - 1):
                        wv_split(c + 1, (c + 1) % 2, kk, c + 1)
                else:
                    w_split(0, 0, None, 0)
                    for k in range(KT - 2):
                        x_split(k)
                if c == RAW:
                    act.wait_ge(col_dve, 5)
                for t in range(0, TT, 2):
                    if c == QUADS - 1 and t in (2, 4):
                        x_split(KT - 3 + t // 2)
                    act.wait_ge(v_ready, c * TT + t + 1)
                    A(vo[:, 2 * c:2 * c + 2, t * P:(t + 1) * P], ps[:, t, 0:2 * P].rearrange("p (a n) -> p a n", a=2),
                      ACT.Copy, scale=col[:, 1, t:t + 1] if c >= RAW else 1.0)
                    A(fl[:, t, 4 * c:4 * c + 4], ps[:, t, 2 * P:VC], ACT.Copy,
                      scale=col[:, 1, t:t + 1] if c >= RAW else 1.0).then_inc(v_used_act, 1)
                if c == QUADS - 2:
                    act.wait_ge(rstd_spread, 1)
                    A(rstd_x[:, half(1)], ps[:, 3, :], ACT.Copy).then_inc(rstd_set, 1)
                if c + 1 < QUADS:
                    wv_split(c + 1, (c + 1) % 2, KT // 2 - 1, c + 1)

            w_split(1, 1, None, 0)
            act.wait_ge(gate_dve, 2)
            A(gate_work[2], gate_work[2], ACT.Exp).then_inc(gate_act, 1)
            act.wait_ge(gate_act, 1)
            A(gate_work[3], gate_work[2], ACT.Ln, bias=1.0).then_inc(gate_act, 1)

            def block_split(pr, par, b, bank):
                act.wait_ge(block_ready, pr * QK_BLOCKS + b + 1)
                A(qk[:, par, 2 * (b // 2), (b % 2) * HALF:(b % 2 + 1) * HALF], ps[:, bank, :], ACT.Copy).then_inc(block_hi, 1)

            for b in range(QK_BLOCKS):
                block_split(0, 0, b, BLOCK_BANK[b])
                if b == 1:
                    w_split(2, 0, block_ready, 2)

            def exp(pr, j, r):
                act.wait_ge(logits_set, pr * 2 * TT + 2 * j + r + 1)
                A(lp_at(r, j), lp_at(r, j), ACT.Exp, scale=-1.0, bias=nmax[:, 2 * j + r:2 * j + r + 1],
                  accum_out=rsum[:, 2 * j + r:2 * j + r + 1]).then_inc(probs_set, 1)

            def turned_hi(pr, n):
                act.wait_ge(turned, pr * NCH + n + 1)
                if not isinstance(pr, int) or pr * NCH + n >= 2:
                    act.wait_ge(pv_done, pr * NCH + n - 1)
                A(turned_at(n, 0), ps[:, TB + n % 2, 0:blocks_of(n) * P], ACT.Copy).then_inc(pt_hi, 1)

            def o_copy(pr, n):
                g, r, c = CHUNKS[n]
                if c < g:
                    return
                unit = pr * UNITS + 2 * g + r
                act.wait_ge(pv_done, pr * NCH + n + 1)
                if not isinstance(pr, int) or unit >= 2:
                    act.wait_ge(o_added, unit - 1)
                head = slice(HD * r, HD * r + HD)
                A(oc[head, 0, :], ps[0:HD, OB, 0:GW], ACT.Copy)
                A(oc[head, 1, :], ps[HD:P, OB, 0:GW], ACT.Copy).then_inc(o_copied, 1)

            def v_split(pr, first):
                if not first:
                    act.wait_ge(pv_done, pr * NCH)
                for t0, t1 in ((0, 2), (2, TT)):
                    src = vo[:, bass.ds(pr, 1), t0 * P:t1 * P].rearrange("p o (s d) -> p (o s) d", d=HD)
                    wait_apart(act, act_passed)
                    A(vs[:, t0:t1, :, 0:HD].rearrange("p t r d -> p (t r) d"), src, ACT.Copy).then_inc(vs_hi, 1)

            def step(pr, par, first=False):
                for what, *a in step_order(first):
                    if what == "logits":
                        if a[0] == 2:
                            v_split(pr, first)
                        if a[0] == 3:
                            w_split(pr * 2 + 3, 1, block_ready, (pr + 1) * QK_BLOCKS)
                        if a[0] == 5:
                            w_split(pr * 2 + 4, 0, block_ready, (pr + 1) * QK_BLOCKS + 2)
                    elif what == "exp":
                        exp(pr, *a)
                    elif what == "turn":
                        turned_hi(pr - a[0], a[1])
                    elif what == "block":
                        block_split(pr + 1, 1 - par, a[0], PB)
                    elif what == "weigh":
                        o_copy(pr - a[0], a[1])

            act.wait_ge(v_used_dve, QUADS * TT // 2)
            act.wait_ge(v_used_act, QUADS * TT // 2)
            act.wait_ge(raw_scaled, 3)
            step(0, 0, first=True)
            with act.Fori(0, (PAIRS - 2) // 2) as i:
                step(i * 2 + 1, 1)
                step(i * 2 + 2, 0)
            step(PAIRS - 1, (PAIRS - 1) % 2)
            w_split(U0 + 1, 1, block_ready, (PAIRS + 1) * QK_BLOCKS)

            def unit_weights(v, par):
                act.wait_ge(unit_ready, v + 1)
                w_split(v + (U0 + 2), par, None, 0)

            def sigmoid_z(src, par, item):
                if not (isinstance(item, int) and item < 2):
                    act.wait_ge(oz_set, item - 1)
                A(work[par], src, ACT.Sigmoid).then_inc(z_sig, 1)

            def z_unit(c, par, n):
                v = c + (n * ZU - AHEAD)
                unit_weights(v, par)
                sigmoid_z(ps[:, par, :], par, z_item(v))

            for what, *a in TAIL:
                if what == "turn":
                    turned_hi(PAIRS - 1, a[1])
                elif what == "weigh":
                    o_copy(PAIRS - 1, a[1])
                    if a[1] == UNIT_0_DONE:
                        unit_weights(0, 0)
                    if a[1] == UNIT_0_DONE + 1:
                        sigmoid_z(ps[:, 0, :], 0, 0)

            def split_pair(n, i, done):
                for k in (2 * i, 2 * i + 1):
                    if done is x1_hi:
                        act.wait_ge(x1_set, n * KT + k + 1)
                    A(xh[:, k, half(n)], vo[:, k, half(n)], ACT.Copy).then_inc(done, 1)

            def joined(i):
                act.wait_ge(z_joined, i + 1)
                sigmoid_z(x_res[i % 2], i % 2, JOINED_AT[i])

            z_order(lambda v: z_unit(v + AHEAD, v % 2, 0), joined)
            for k in range(PK):
                z_unit(AHEAD + k, k % 2, 1)
                act.wait_ge(p_in[k], 16)
                A(p_sp[:, 0, k, :], cb[:, k, :], ACT.Copy).then_inc(p_hi, 1)
            act.wait_ge(oz_set, len(JOINED) + ZU)
            for i in range(KT // 2):
                split_pair(0, i, oz_hi)
                z_unit(KT // 2 + i, i % 2, 1)

            act.wait_ge(oz_set, len(JOINED) + 2 * ZU)

            def y_unit(c, par, n):
                unit_weights(c + (V_Y + n * KT), par)
                if later(c, n):
                    act.wait_ge(sq_added, c + (n * KT - 1))
                A(work[par], ps[:, par, :], ACT.Square).then_inc(sq_set, 1)
                wait_apart(act, act_passed)
                A(o_tile(c, n), ps[:, par, :], ACT.Copy, scale=g_post_sb[:, bass.ds(c, 1)]).then_inc(y_set, 1)

            for c in range(2):
                y_unit(c, c, 0)
            units(act, lambda c, par: y_unit(c, par, 0), 2, KT // 2)
            for i in range(KT // 2):
                split_pair(1, i, oz_hi)
                y_unit(KT // 2 + i, i % 2, 0)
            y_unit(0, 0, 1)
            root(1, HT)
            y_unit(1, 1, 1)
            units(act, lambda c, par: y_unit(c, par, 1), 2, KT // 2)

            def ple_split(c, par, n):
                act.wait_ge(ple_in[par], (c - par + (n * KT + 2)) * 8)
                if later(c, n):
                    act.wait_ge(ple_ready, c + (n * KT - 1))
                A(ple_sp[:, par, 0, :], ple_raw[par], ACT.Copy).then_inc(ple_hi, 1)

            for c in range(2):
                ple_split(c, c, 0)
            for i in range(KT // 2):
                split_pair(0, i, x1_hi)
                y_unit(KT // 2 + i, i % 2, 1)

            def g_weights(c, par, n):
                unit_weights(c + (V_G + n * KT), par)
                if isinstance(c, int) and c >= KT - 2:
                    ple_split(c + 2 - KT, par, n + 1)
                else:
                    ple_split(c + 2, par, n)

            def g_unit(c, par, n):
                if later(c, n):
                    act.wait_ge(out_done[par], (c - par + n * KT) * 8)
                else:
                    act.wait_ge(sq_added, 2 * KT)
                wait_apart(act, act_passed)
                A(work[par], ps[:, par, :], ACT.Sigmoid,
                  bias=b_gate_sb[:, bass.ds(c, 1)]).then_inc(g_sig, 1)

            def g_both(c, par, n):
                g_weights(c, par, n)
                g_unit(c, par, n)

            g_weights(0, 0, 0)
            root(2, HT)
            g_unit(0, 0, 0)
            g_both(1, 1, 0)
            units(act, lambda c, par: g_both(c, par, 0), 2, KT // 2)
            for i in range(KT // 2):
                split_pair(1, i, x1_hi)
                g_both(KT // 2 + i, i % 2, 0)
            units(act, lambda c, par: g_both(c, par, 1), 0, KT - 2)
            for c in (KT - 2, KT - 1):
                act.wait_ge(unit_ready, V_G + KT + c + 1)
                g_unit(c, c % 2, 1)

        @block.vector
        def _(dve):
            tt, ts, stt = nc.vector.tensor_tensor, nc.vector.tensor_scalar, nc.vector.scalar_tensor_tensor

            def lo(out, whole, hi, done):
                tt(out, whole, f32(hi), ALU.subtract).then_inc(done, 1)

            def factors(which, sums, count):
                n, tiles = which * 5, TT if which == 0 else HT
                mean, factor, work_ = (col[:, i, 0:tiles] for i in range(3))
                dve.wait_ge(sum_ready, count)
                ts(mean, sums, 1.0 / D, EPS, ALU.mult, ALU.add).then_inc(col_dve, 1)
                dve.wait_ge(col_act, which * 2 + 2)
                tt(work_, factor, factor, ALU.mult).then_inc(col_dve, 1)
                dve.wait_ge(col_dve, n + 2)
                tt(work_, work_, mean, ALU.mult).then_inc(col_dve, 1)
                dve.wait_ge(col_dve, n + 3)
                ts(work_, work_, -0.5, 1.5, ALU.mult, ALU.add).then_inc(col_dve, 1)
                dve.wait_ge(col_dve, n + 4)
                tt(factor, factor, work_, ALU.mult).then_inc(col_dve, 1)
                dve.wait_ge(col_dve, n + 5)
                dve.wait_ge(const_set, 4)
                tt(diag[:, 0:tiles, :], ident[:, None, :].to_broadcast([P, tiles, P]),
                   factor[:, :, None].to_broadcast([P, tiles, P]), ALU.mult).then_inc(diag_set, 1)

            dve.wait_ge(vecs_in, 16)

            def wv_lo_part(c, kk):
                dve.wait_ge(wv_hi, c * (KT // 2) + kk + 1)
                k = slice(2 * kk, 2 * kk + 2)
                lo(wv_sp[:, k, 1, :], wv_raw[c % 2][:, k, :], wv_sp[:, k, 0, :], wv_lo)

            def x_first_lo(k, tokens):
                stt(out=xl[:, k, tokens], in0=vo[:, k, tokens], scalar=g_pre_sb[:, k:k + 1], in1=f32(xh[:, k, tokens]),
                    op0=ALU.mult, op1=ALU.subtract).then_inc(x0_lo if tokens == half(0) else x_lo, 1)

            dve.wait_ge(x0_hi, 1)
            x_first_lo(0, half(0))
            wv_lo_part(0, 0)
            for k in range(KT):
                dve.wait_ge(x_hi, k + 1)
                x_first_lo(k, slice(0 if k else HALF, T))
                if k and k % 2 == 0:
                    wv_lo_part(0, k // 2)

            def x_scale(k):
                dve.wait_ge(x_summed, k + 1)
                tt(x_sum[k % 3], x_sum[k % 3], rstd_x, ALU.mult).then_inc(x_scaled, 1)

            def x_rest(k):
                dve.wait_ge(x_hi, KT + k + 1)
                lo(xl[:, k, :], x_sum[k % 3], xh[:, k, :], x_lo)

            for c in range(QUADS):
                if c == QUADS - 1:
                    dve.wait_ge(rstd_set, 2)
                if c == RAW:
                    factors(0, ps[:, 0, 0:TT], 1)
                    dve.wait_ge(v_used_act, RAW * TT // 2)
                    dve.wait_ge(v_used_dve, RAW * TT // 2)
                    scales = col[:, 1, :][:, None, :, None]
                    for part in range(RAW):
                        v = vo[:, 2 * part:2 * part + 2, :].rearrange("p a (t n) -> p a t n", t=TT)
                        tt(v, v, scales.to_broadcast([P, 2, TT, P]), ALU.mult).then_inc(raw_scaled, 1)
                    gates = fl[:, :, 0:4 * RAW]
                    tt(gates, gates, col[:, 1, :][:, :, None].to_broadcast([P, TT, 4 * RAW]), ALU.mult).then_inc(raw_scaled, 1)
                if c == QUADS - 1:
                    for k in range(KT - 1):
                        if k < KT - 2:
                            x_scale(k)
                        if k:
                            x_rest(k - 1)
                if c + 1 < QUADS:
                    for kk in range(KT // 2 - 1):
                        wv_lo_part(c + 1, kk)
                for t in range(1, TT, 2):
                    if c == QUADS - 1 and t == 1:
                        x_scale(KT - 2)
                    if c == QUADS - 1 and t == 3:
                        x_scale(KT - 1)
                        x_rest(KT - 2)
                    if c == QUADS - 1 and t == 5:
                        x_rest(KT - 1)
                    dve.wait_ge(v_ready, c * TT + t + 1)
                    scale_v = col[:, 1, t:t + 1] if c >= RAW else 1.0
                    ts(vo[:, 2 * c:2 * c + 2, t * P:(t + 1) * P], ps[:, t, 0:2 * P].rearrange("p (a n) -> p a n", a=2),
                       scale_v, None, ALU.mult)
                    ts(fl[:, t, 4 * c:4 * c + 4], ps[:, t, 2 * P:VC], scale_v, None, ALU.mult).then_inc(v_used_dve, 1)
                if c == QUADS - 2:
                    dve.wait_ge(rstd_spread, 1)
                    nc.vector.tensor_copy(rstd_x[:, half(0)], ps[:, 2, :]).then_inc(rstd_set, 1)
                if c + 1 < QUADS:
                    wv_lo_part(c + 1, KT // 2 - 1)

            w0, w1, w2, w3 = gate_work
            dve.wait_ge(bf_in, 16)
            dve.wait_ge(fl_turned, 1)
            ts(w1, ps[0:HEADS, FB:FB + 2, :].rearrange("p b n -> p (b n)"), bf[:], None, ALU.add).then_inc(gate_dve, 1)
            dve.wait_ge(gate_dve, 1)
            stt(out=w2, in0=w1, scalar=-1.0, in1=w1, op0=ALU.mult, op1=ALU.min).then_inc(gate_dve, 1)
            dve.wait_ge(gate_act, 2)
            stt(out=w2, in0=w1, scalar=0.0, in1=w3, op0=ALU.min, op1=ALU.subtract).then_inc(gate_dve, 1)
            nc.vector.memset(w0, 1.0).then_inc(gate_dve, 1)
            dve.wait_ge(gate_dve, 4)
            nc.vector.tensor_tensor_scan(w1, w0, w2, 0.0, ALU.mult, ALU.add).then_inc(gate_dve, 1)
            dve.wait_ge(gate_dve, 5)
            ts(w0, w1, -1.0 / SCALE, None, ALU.mult).then_inc(gate_dve, 1)

            def block_rest(pr, par, b, bank):
                dve.wait_ge(block_hi, pr * QK_BLOCKS + b + 1)
                lo(qk[:, par, 2 * (b // 2) + 1, half(b % 2)], ps[:, bank, :], qk[:, par, 2 * (b // 2), half(b % 2)], block_lo)

            for b in range(QK_BLOCKS):
                block_rest(0, 0, b, BLOCK_BANK[b])

            def take(pr, j, r, first):
                w, nb = key_width(j)
                if j == 0 and r == 0:
                    dve.wait_ge(cb_in, (pr + 1) * 32)
                if j >= PLACES:
                    dve.wait_ge(turned, pr * NCH + chunks_until((j - PLACES) // 2, r))
                elif not first:
                    dve.wait_ge(turned, (pr - 1) * NCH + chunks_until((j + PLACES) // 2, r))
                dve.wait_ge(logits_ready, pr * 2 * TT + 2 * j + r + 1)
                wait_apart(dve, dve_passed)
                src = ps[:, SB + 2 * r:SB + 2 * r + nb, 0:w // nb]
                nc.vector.tensor_tensor_reduce(
                    out=lp_at(r, j).rearrange("p (b n) -> p b n", b=nb), in0=src,
                    in1=cb[:, r, 0:w].rearrange("p (b n) -> p b n", b=nb), scale=-SCALE, scalar=BIG,
                    op0=ALU.add, op1=ALU.min, accum_out=nmax[:, 2 * j + r:2 * j + r + 1]).then_inc(logits_set, 1)

            def scale(pr, j, r):
                n = 2 * j + r
                dve.wait_ge(probs_set, pr * 2 * TT + n + 1)
                nc.vector.reciprocal(rinv[:, n:n + 1], rsum[:, n:n + 1]).then_inc(sums_inverted, 1)
                dve.wait_ge(sums_inverted, pr * 2 * TT + n + 1)
                ts(lp_at(r, j), lp_at(r, j), rinv[:, n:n + 1], None, ALU.mult).then_inc(probs_scaled, 1)

            def turned_lo(pr, n):
                dve.wait_ge(pt_hi, pr * NCH + n + 1)
                lo(turned_at(n, 1), ps[:, TB + n % 2, 0:blocks_of(n) * P], turned_at(n, 0), pt_lo)

            def step(pr, par, first=False):
                for what, *a in step_order(first):
                    if what == "take":
                        take(pr, *a, first)
                    elif what == "scale":
                        scale(pr - a[0], a[1], a[2])
                    elif what == "turn":
                        turned_lo(pr - a[0], a[1])
                    elif what == "block":
                        block_rest(pr + 1, 1 - par, a[0], PB)

            step(0, 0, first=True)
            with dve.Fori(0, (PAIRS - 2) // 2) as i:
                step(i * 2 + 1, 1)
                step(i * 2 + 2, 0)
            step(PAIRS - 1, (PAIRS - 1) % 2)
            def gate_z(z, par, item):
                dve.wait_ge(z_sig, item + 1)
                tt(work[par], z, work[par], ALU.mult).then_inc(z_mul, 1)

            for what, *a in TAIL:
                if what == "turn":
                    turned_lo(PAIRS - 1, a[1])
                elif what == "scale":
                    scale(PAIRS - 1, a[1], a[2])
                elif what == "weigh" and a[1] == UNIT_0_DONE + 1:
                    gate_z(ps[:, 0, :], 0, 0)

            def joined(i):
                n, c = JOINED[i]
                if i == 0:
                    dve.wait_ge(turned, PAIRS * NCH)
                    dve.wait_ge(block_lo, (PAIRS + 1) * QK_BLOCKS)
                if i >= 2:
                    dve.wait_ge(z_mul, JOINED_AT[i - 2] + 1)
                tt(x_res[i % 2], f32(qk[:, 0, 2 * c, half(n)]), f32(qk[:, 0, 2 * c + 1, half(n)]), ALU.add).then_inc(z_joined, 1)
                dve.wait_ge(z_joined, i + 1)
                gate_z(x_res[i % 2], i % 2, JOINED_AT[i])

            z_order(lambda v: gate_z(ps[:, v % 2, :], v % 2, z_item(v)), joined)

            def split_pair(n, i, hi_done, done):
                for k in (2 * i, 2 * i + 1):
                    dve.wait_ge(hi_done, n * KT + k + 1)
                    lo(xl[:, k, half(n)], vo[:, k, half(n)], xh[:, k, half(n)], done)

            def z_unit(c, par, n):
                gate_z(ps[:, par, :], par, z_item(c + (n * ZU - AHEAD)))

            for k in range(PK):
                z_unit(AHEAD + k, k % 2, 1)
                dve.wait_ge(p_hi, k + 1)
                lo(p_sp[:, 1, k, :], cb[:, k, :], p_sp[:, 0, k, :], p_lo)
            for i in range(KT // 2):
                split_pair(0, i, oz_hi, oz_lo)
                z_unit(KT // 2 + i, i % 2, 1)

            dve.wait_ge(p_lo, PK)

            def y_unit(c, par, n):
                dve.wait_ge(sq_set, c + (n * KT + 1))
                sums = sq_sum[:, half(n)]
                if isinstance(c, int) and c == 0:
                    nc.vector.tensor_copy(sums, work[par]).then_inc(sq_added, 1)
                else:
                    dve.wait_ge(sq_added, c + n * KT)
                    tt(sums, sums, work[par], ALU.add).then_inc(sq_added, 1)

            def spread_norm(n):
                dve.wait_ge(rstd_spread, n + 2)
                nc.vector.tensor_copy(rstd_y[:, half(n)], ps[:, 7, :]).then_inc(rstd_set, 1)
                dve.wait_ge(rstd_set, n + 3)

            def x1_pair(n, i):
                for k in (2 * i, 2 * i + 1):
                    y = vo[:, k, half(n)]
                    dve.wait_ge(y_set, n * KT + k + 1)
                    tt(y, y, rstd_y[:, half(n)], ALU.mult).then_inc(x1_scaled, 1)
                split_pair(n, i, x1_hi, x1_lo)

            for c in range(2):
                y_unit(c, c, 0)
            units(dve, lambda c, par: y_unit(c, par, 0), 2, KT // 2)
            for i in range(KT // 2):
                split_pair(1, i, oz_hi, oz_lo)
                y_unit(KT // 2 + i, i % 2, 0)
            y_unit(0, 0, 1)
            factors(1, ps[:, 6, 0:HT], 2)
            y_unit(1, 1, 1)
            y_unit(2, 0, 1)
            spread_norm(0)
            y_unit(3, 1, 1)

            def ple_split(c, par, n):
                dve.wait_ge(ple_hi, c + (n * KT + 1))
                lo(ple_sp[:, par, 1, :], ple_raw[par], ple_sp[:, par, 0, :], ple_lo)

            for c in range(2):
                ple_split(c, c, 0)
            for i in range(KT // 2):
                x1_pair(0, i)
                y_unit(KT // 2 + i, i % 2, 1)

            def g_unit(c, par, n, more=True):
                if not more:
                    pass
                elif isinstance(c, int) and c >= KT - 2:
                    ple_split(c + 2 - KT, par, n + 1)
                else:
                    ple_split(c + 2, par, n)
                dve.wait_ge(ple_ready, c + (n * KT + 1))
                dve.wait_ge(g_sig, c + (n * KT + 1))
                tt(work[par], ps[:, 2 + par, :], work[par], ALU.mult).then_inc(g_mul, 1)
                dve.wait_ge(g_mul, c + (n * KT + 1))
                tt(work[par], work[par], o_tile(c, n), ALU.add).then_inc(g_add, 1)

            factors(2, ps[:, 6, HT:TT], 3)
            for c in range(3):
                g_unit(c, c % 2, 0)
            spread_norm(1)
            g_unit(3, 1, 0)
            for i in range(KT // 2):
                x1_pair(1, i)
                g_unit(KT // 2 + i, i % 2, 0)
            units(dve, lambda c, par: g_unit(c, par, 1), 0, KT - 2)
            for c in (KT - 2, KT - 1):
                g_unit(c, c % 2, 1, more=False)


def chunks_of_columns(w):
    k, n = w.shape
    return np.ascontiguousarray(w.reshape(k // P, P, n // P, P).transpose(2, 1, 0, 3).reshape(n // P, P, k))


def kernel(**inputs):
    import concourse.bacc as bacc
    from concourse.bass_utils import run_bass_kernel_spmd

    a = {k: np.asarray(v) for k, v in inputs.items()}
    x, w_in = a["x"][0], a["fox_w_in"][0]
    wq, wk, wv, wz, wf = np.split(w_in, [D, 2 * D, 3 * D, 4 * D], axis=1)
    wv = np.concatenate([wv.reshape(D, QUADS, 4 * HD), wf.reshape(D, QUADS, 4)], axis=2)
    wv = np.ascontiguousarray(wv.reshape(KT, P, QUADS, VC).transpose(2, 1, 0, 3))
    q, k = chunks_of_columns(wq), chunks_of_columns(wk)
    qk = np.stack([q, k], axis=1).reshape(2 * PAIRS, P, D)
    w_all = np.concatenate([qk, chunks_of_columns(wz), chunks_of_columns(a["fox_w_out"][0]),
                            chunks_of_columns(a["ple_w_gate"][0])])
    vectors = np.stack([a[n][0].reshape(KT, P).T for n in ("ln_pre", "ln_post", "ple_b_gate")], axis=1)
    arrays = {
        "x_t": np.ascontiguousarray(x.T).reshape(KT, P, T),
        "wv": wv,
        "w_all": w_all,
        "w_ple": chunks_of_columns(a["ple_w_proj"][0]),
        "p_t": np.ascontiguousarray(a["p"][0, 0].T).reshape(PK, P, T),
        "f_bias": np.ascontiguousarray(a["fox_b_f"][0].reshape(HEADS, 1)),
        "vectors": np.ascontiguousarray(vectors),
    }
    nc = bacc.Bacc("TRN2", target_bir_lowering=False, num_devices=1)
    aps = {n: nc.dram_tensor(n, v.shape, F32, kind="ExternalInput").ap() for n, v in arrays.items()}
    scratch = nc.dram_tensor("scratch", (HEADS, T), F32, kind="Internal").ap()
    out_t = nc.dram_tensor("out_t", (KT, P, T), F32, kind="ExternalOutput").ap()
    build(nc, **aps, scratch=scratch, out_t=out_t)
    r = run_bass_kernel_spmd(nc, [arrays], core_ids=[0])
    out = r.results[0]["out_t"]
    return np.ascontiguousarray(out.reshape(D, T).T).reshape(1, T, D)
```
